# Optimizing a Trainium2 kernel written in Bass

```python
import math
import jax, jax.numpy as jnp
from jax import lax
import numpy as np

D_MODEL = 1024
BATCH = 1
SEQ = 512
DEPTH = 1

CHUNK = 64
D_MIX = D_MODEL
D_POOL = D_MIX // 2
D_LRU = D_MIX - D_POOL
POOL_WINDOWS = (2, 4, 8, 16)
POOL_GROUPS = len(POOL_WINDOWS)
POOL_GW = D_POOL // POOL_GROUPS
LRU_HEADS = 8
LRU_HD = D_LRU // LRU_HEADS
CONV_W = 4
LRU_C = 8.0
PEER_HEADS = 8
PEER_NKEYS = 128
PEER_N = PEER_NKEYS * PEER_NKEYS
PEER_DKEY = 256
PEER_TOPK = 16
PEER_BLOCK = 128
LN_EPS = 1e-5
ALPHA = (2.0 * DEPTH) ** 0.25
BETA = (8.0 * DEPTH) ** -0.25

kernel_name = "hybrid_pool_rglru_peer_deepnorm_adaln"

def layer_norm(x, g, b):
    xf = x.astype(jnp.float32)
    mu = jnp.mean(xf, axis=-1, keepdims=True)
    var = jnp.mean(jnp.square(xf - mu), axis=-1, keepdims=True)
    y = (xf - mu) * lax.rsqrt(var + LN_EPS)
    return (y * g.astype(jnp.float32) + b.astype(jnp.float32)).astype(x.dtype)

def pool_mixer(p, w_grp, scale):
    B, S, _ = p.shape
    pf = p.astype(jnp.float32).reshape(B, S, POOL_GROUPS, POOL_GW)
    cs = jnp.cumsum(pf, axis=1)
    count = jnp.arange(1, S + 1, dtype=jnp.float32)
    outs = []
    for g, w in enumerate(POOL_WINDOWS):
        cg = cs[:, :, g]
        lag = jnp.pad(cg[:, :S - w], ((0, 0), (w, 0), (0, 0)))
        mean = (cg - lag) / jnp.minimum(count, float(w))[None, :, None]
        outs.append(mean - pf[:, :, g])
    y = jnp.stack(outs, axis=2).astype(p.dtype)
    y = jnp.einsum('bsgi,gij->bsgj', y, w_grp).reshape(B, S, D_POOL)
    return y * scale

def _lin_rec_combine(left, right):
    a1, b1 = left
    a2, b2 = right
    return a1 * a2, a2 * b1 + b2

def rglru_mixer(xr, yg, conv_w, conv_b, wa, ba, wx, bx, lam):
    B, S, _ = xr.shape
    xc = lax.conv_general_dilated(xr, conv_w, window_strides=(1,), padding=((CONV_W - 1, 0),),
                                  dimension_numbers=('NWC', 'WIO', 'NWC'),
                                  feature_group_count=D_LRU) + conv_b
    xh = xc.reshape(B, S, LRU_HEADS, LRU_HD)
    r = jax.nn.sigmoid(jnp.einsum('bshi,hij->bshj', xh, wa) + ba).reshape(B, S, D_LRU)
    i = jax.nn.sigmoid(jnp.einsum('bshi,hij->bshj', xh, wx) + bx).reshape(B, S, D_LRU)
    log_a = -LRU_C * jax.nn.softplus(-lam.astype(jnp.float32)) * r.astype(jnp.float32)
    a = jnp.exp(log_a)
    b = jnp.sqrt(-jnp.expm1(2.0 * log_a)) * (i * xc).astype(jnp.float32)
    _, h = lax.associative_scan(_lin_rec_combine, (a, b), axis=1)
    return h.astype(xr.dtype) * jax.nn.gelu(yg)

def peer(h, w_q, k1, k2, u, v):
    B, S, D = h.shape
    T = B * S
    half = PEER_DKEY // 2
    hf = h.reshape(T, D)
    q = (hf @ w_q).reshape(T, PEER_HEADS, PEER_DKEY).astype(jnp.float32)
    q = (q - jnp.mean(q, -1, keepdims=True)) * lax.rsqrt(jnp.var(q, -1, keepdims=True) + LN_EPS)
    s1 = jnp.einsum('thd,nd->thn', q[..., :half], k1.astype(jnp.float32))
    s2 = jnp.einsum('thd,nd->thn', q[..., half:], k2.astype(jnp.float32))
    v1, i1 = lax.top_k(s1, PEER_TOPK)
    v2, i2 = lax.top_k(s2, PEER_TOPK)
    cand = (v1[..., :, None] + v2[..., None, :]).reshape(T, PEER_HEADS, PEER_TOPK * PEER_TOPK)
    vs, j = lax.top_k(cand, PEER_TOPK)
    e = (jnp.take_along_axis(i1, j // PEER_TOPK, axis=-1) * PEER_NKEYS
         + jnp.take_along_axis(i2, j % PEER_TOPK, axis=-1))
    g = jax.nn.softmax(vs, axis=-1).astype(h.dtype)
    nb = T // PEER_BLOCK
    hk = PEER_HEADS * PEER_TOPK
    xb_all = hf.reshape(nb, PEER_BLOCK, D)
    eb_all = e.reshape(nb, PEER_BLOCK, hk)
    gb_all = g.reshape(nb, PEER_BLOCK, hk)

    def block(args):
        xb, eb, gb = args
        act = jax.nn.gelu(jnp.einsum('td,tkd->tk', xb, u[eb]))
        return jnp.einsum('tk,tkd->td', gb * act, v[eb])

    out = lax.map(block, (xb_all, eb_all, gb_all))
    return out.reshape(B, S, D)

def setup_inputs(seed: int = 0) -> dict:
    key = jax.random.key(seed)
    ks = jax.random.split(key, 32)
    f32 = jnp.float32
    D = D_MODEL
    L = DEPTH

    def nrm(k, shape, s):
        return jax.random.normal(k, shape, f32) * s

    gate_slots = jnp.repeat(jnp.array([0.0, 0.0, 1.0, 0.0, 0.0, 1.0], f32), D)
    a_c = jax.random.uniform(ks[15], (L, D_LRU), f32, 0.9, 0.999)
    a0 = a_c ** (1.0 / LRU_C)
    return {
        "x": nrm(ks[0], (BATCH, SEQ, D), 1.0),
        "c": nrm(ks[1], (BATCH, D), 1.0),
        "ln0_g": 1.0 + nrm(ks[2], (D,), 0.02),
        "ln0_b": nrm(ks[3], (D,), 0.02),
        "ada_w": nrm(ks[4], (L, D, 6 * D), 0.2 * D ** -0.5),
        "ada_b": gate_slots + nrm(ks[5], (L, 6 * D), 0.02),
        "w_in": nrm(ks[6], (L, D, D_POOL + 2 * D_LRU), D ** -0.5),
        "pool_w": nrm(ks[7], (L, POOL_GROUPS, POOL_GW, POOL_GW), POOL_GW ** -0.5),
        "pool_scale": 1.0 + nrm(ks[8], (L, D_POOL), 0.02),
        "conv_w": nrm(ks[9], (L, CONV_W, 1, D_LRU), CONV_W ** -0.5),
        "conv_b": nrm(ks[10], (L, D_LRU), 0.02),
        "lru_wa": nrm(ks[11], (L, LRU_HEADS, LRU_HD, LRU_HD), LRU_HD ** -0.5),
        "lru_ba": nrm(ks[12], (L, LRU_HEADS, LRU_HD), 0.02),
        "lru_wx": nrm(ks[13], (L, LRU_HEADS, LRU_HD, LRU_HD), LRU_HD ** -0.5),
        "lru_bx": nrm(ks[14], (L, LRU_HEADS, LRU_HD), 0.02),
        "lru_lambda": jnp.log(a0) - jnp.log1p(-a0),
        "w_out": nrm(ks[16], (L, D_MIX, D), BETA * D_MIX ** -0.5),
        "ln1_g": 1.0 + nrm(ks[17], (L, D), 0.02),
        "ln1_b": nrm(ks[18], (L, D), 0.02),
        "peer_wq": nrm(ks[19], (L, D, PEER_HEADS * PEER_DKEY), D ** -0.5),
        "peer_k1": nrm(ks[20], (L, PEER_NKEYS, PEER_DKEY // 2), (PEER_DKEY // 2) ** -0.5),
        "peer_k2": nrm(ks[21], (L, PEER_NKEYS, PEER_DKEY // 2), (PEER_DKEY // 2) ** -0.5),
        "peer_u": nrm(ks[22], (L, PEER_N, D), D ** -0.5),
        "peer_v": nrm(ks[23], (L, PEER_N, D), BETA),
        "ln2_g": 1.0 + nrm(ks[24], (L, D), 0.02),
        "ln2_b": nrm(ks[25], (L, D), 0.02),
    }

def reference(x, c, ln0_g, ln0_b, ada_w, ada_b, w_in, pool_w, pool_scale, conv_w, conv_b,
              lru_wa, lru_ba, lru_wx, lru_bx, lru_lambda, w_out, ln1_g, ln1_b,
              peer_wq, peer_k1, peer_k2, peer_u, peer_v, ln2_g, ln2_b):
    x = layer_norm(x, ln0_g, ln0_b)
    cond = jax.nn.silu(c)
    for l in range(DEPTH):
        mod = cond @ ada_w[l] + ada_b[l]
        sh1, sc1, g1, sh2, sc2, g2 = [m[:, None, :] for m in jnp.split(mod, 6, axis=-1)]
        h = x * (1.0 + sc1) + sh1
        z = h @ w_in[l]
        zp = z[..., :D_POOL]
        zx = z[..., D_POOL:D_POOL + D_LRU]
        zg = z[..., D_POOL + D_LRU:]
        y_pool = pool_mixer(zp, pool_w[l], pool_scale[l])
        y_lru = rglru_mixer(zx, zg, conv_w[l], conv_b[l], lru_wa[l], lru_ba[l],
                            lru_wx[l], lru_bx[l], lru_lambda[l])
        y = jnp.concatenate([y_pool, y_lru], axis=-1) @ w_out[l]
        x = layer_norm(ALPHA * x + g1 * y, ln1_g[l], ln1_b[l])
        h = x * (1.0 + sc2) + sh2
        y = peer(h, peer_wq[l], peer_k1[l], peer_k2[l], peer_u[l], peer_v[l])
        x = layer_norm(ALPHA * x + g2 * y, ln2_g[l], ln2_b[l])
    return x


_drawn_inputs = setup_inputs


def setup_inputs(seed=0):
    import zlib

    import numpy as np

    out = dict(_drawn_inputs(seed))
    spreads = {}
    factors = {'lru_ba': 19.445, 'lru_bx': 5.725, 'ln2_g': 8.167, 'ln2_b': 8.021, 'pool_scale': 2.791}
    for name, (base, spread) in spreads.items():
        noise = np.random.default_rng([zlib.crc32(name.encode()), seed]).standard_normal(out[name].shape)
        drawn = base * np.exp(spread * noise) if base else spread * noise
        out[name] = __import__('jax').numpy.asarray(drawn.astype(out[name].dtype))
    for name, factor in factors.items():
        out[name] = (out[name] * factor).astype(out[name].dtype)
    return out
```

```python
from contextlib import ExitStack

import concourse.bass as bass
from concourse import mybir
from concourse.alu_op_type import AluOpType as ALU

F32 = mybir.dt.float32
U32 = mybir.dt.uint32
ACT = mybir.ActivationFunctionType
AX = mybir.AxisListType

P = 128
D = 1024
KD = D // P
S = 512
TB = S // P
NMOD = 6
WINDOWS = (2, 4, 8, 16)
NG = len(WINDOWS)
CONV_W = 4
H = 8
DK = 256
NK = 128
K = 16
PICKS = H * K
CHUNK_C = 512
PIECES = ([("ada", j) for j in range(4)] + [("win", 1), ("win", 0), ("win", 2)]
          + [("ada", j) for j in range(4, 11)] + [("wout", 0), ("wout", 1)]
          + [("wq", j) for j in range(4)] + [("ada", 11)])
SLOTS = 4
CAND_A = 4 * K
CAND = CAND_A + (K - 4) * 4
LN_EPS = 1e-5
ALPHA = 2.0 ** 0.25
LRU_C = 8.0
DROPPED = -3.0e38
PAD_P = max(WINDOWS)
PAD_C = 4
GT = 4
NT = NK
TOK = 16

COLS = {}
_n = 0
for _name, _w in (("c", 8), ("ada_b", 48), ("ln0_g", 8), ("ln0_b", 8), ("ln1_g", 8), ("ln1_b", 8),
                  ("pool_scale", 4), ("conv_b", 4), ("lru_ba", 4), ("lru_bx", 4), ("lam", 4),
                  ("conv_w", 16)):
    COLS[_name] = (_n, _n + _w)
    _n += _w
NCOLS = _n
ROWS = ("ln0_g", "ln0_b", "ln1_g", "ln1_b", "ln2_g", "ln2_b")
C_ID, C_IOTA, C_ONE, C_MEAN, C_EPS, C_CNT = 0, P, 2 * P, 3 * P, 3 * P + 1, 3 * P + 2
NCONST = C_CNT + NG * PAD_P


class Chain:

    def __init__(self, eng, sem, reg=None, per=0):
        self.eng, self.sem, self.reg, self.per, self.n = eng, sem, reg, per, 0

    def link(self, ins):
        ins.then_inc(self.sem, 1)
        self.n += 1
        self.eng.wait_ge(self.sem, self.n if self.reg is None else self.reg * self.per + self.n)


def build(nc, x, cols, rows, consts, ada_w, w_in, w_out, wq, pool_w, wa, wx, k1t, k2t, ut, v, out):
    ctx = ExitStack()
    with ctx:
        def sb(name, shape, dt=F32):
            return ctx.enter_context(nc.sbuf_tensor(name, shape, dt))

        def sem(name):
            return ctx.enter_context(nc.semaphore(name))

        gates = nc.dram_tensor("gates_dram", [NT, P, S], F32, kind="Internal").ap()

        bank = [ctx.enter_context(nc.psum_tensor(f"bank{i}", [P, 512], F32)) for i in range(8)]
        hT = sb("hT", [P, KD, S])
        xt = sb("xt", [P, TB, D])
        wbuf = sb("wbuf", [P, SLOTS * KD * CHUNK_C])
        row_g = sb("row_g", [P, D])
        row_b = sb("row_b", [P, D])
        row_gate = sb("row_gate", [P, D])
        cst = sb("cst", [P, NCONST])
        col = sb("col", [P, NCOLS])
        mod = sb("mod", [P, 48])
        sc = sb("sc", [P, 96])
        st = sb("st", [P, TB, 2, 6])
        mv = sb("mv", [P, TB, 2])
        sd = sb("sd", [P, TB])
        rstd = sb("rstd", [P, TB])
        ramp = sb("ramp", [P, NG, PAD_P])
        hsum = sb("hsum", [P, H, KD])
        hmean = sb("hmean", [P, H, KD])
        ARENA = 23552
        arena = sb("arena", [P, ARENA])

        ident = cst[:, C_ID:C_ID + P]
        iota = cst[:, C_IOTA:C_IOTA + P]
        ones = cst[:, C_ONE:C_ONE + P]
        mean_col = cst[:, C_MEAN:C_MEAN + 1]
        eps = cst[:, C_EPS:C_EPS + 1]
        inv_count = cst[:, C_CNT:C_CNT + NG * PAD_P].rearrange("p (g w) -> p g w", g=NG)

        def vec(name, j=None):
            a, b = COLS[name]
            return col[:, a:b] if j is None else col[:, a + j:a + j + 1]

        silu_c = sc[:, 0:8]
        scale1, bias1, scale2, bias2 = (sc[:, 8 * n:8 * n + 8] for n in (1, 2, 3, 4))
        decay = sc[:, 40:44]
        ndecay = sc[:, 44:48]
        t4 = [sc[:, 48 + 4 * n:52 + 4 * n] for n in range(7)]

        piece_buf = wbuf[:, :].rearrange("p (s k n) -> p s k n", s=SLOTS, k=KD)

        def carve(spec):
            at, got = 0, []
            for shape in spec:
                n = 1
                for w in shape:
                    n *= w
                a = arena[:, at:at + n]
                if len(shape) == 2:
                    a = a.rearrange("p (a b) -> p a b", a=shape[0])
                if len(shape) == 3:
                    a = a.rearrange("p (a b c) -> p a b c", a=shape[0], b=shape[1])
                got.append(a)
                at += n
            assert at <= ARENA, at
            return got

        zp, zx, zg, pa, pb, xc, gr, gi, yT, pw, wab, wxb, diag = carve(
            [(NG, PAD_P + S), (4, PAD_C + S), (4, S), (NG, PAD_P + S), (NG, PAD_P + S), (4, S), (4, S), (4, S),
             (KD, S), (NG, P), (4, P), (4, P), (KD, P)])
        (wqc, qT, sq, keys, e1, e2, wt, vs, s_all, s_val, s_pos, s_posf, cand, c_val, c_idx, dec, eq_a, eq_b,
         pk) = carve(
            [(2, KD, DK), (2, 2, S), (2, 2, S), (2, NK), (TB, PICKS), (TB, PICKS), (TB, PICKS), (TB, PICKS),
             (2, TB, DK), (2, TB, K), (2, TB, K), (2, TB, K), (TB, CAND), (TB, K), (TB, K), (8, TB * K),
             (TB * K, K), (TB * K, K), (4, TB * H)])
        stage_a, i1T, i2T, wT, onehot_w, onehot = carve(
            [(P, P), (S,), (S,), (S,), (TOK, P), (TOK, P)])
        stage = [stage_a, wbuf[:, :].rearrange("p (a b) -> p a b", a=P)]
        acc, ring_w, ring_a, ring_g, tmp = carve([(TB, D), (2 * GT, S), (GT, S), (2 * GT, S), (TB, D // 4)])
        tmp = tmp.rearrange("p a b -> p (a b)")
        ring_u = wbuf[:, 0:8192].rearrange("p (s k n) -> p s k n", s=2 * GT, k=KD)
        ring_v = wbuf[:, 8192:16384].rearrange("p (s n) -> p s n", s=2 * GT)

        s_x = [sem(f"x_landed{n}") for n in range(TB)]
        s_piece = [sem(f"piece_landed{n}") for n in range(SLOTS)]
        s_u = [sem(f"u_landed{n}") for n in range(2 * GT)]
        s_v = [sem(f"v_landed{n}") for n in range(2 * GT)]
        s_g = [sem(f"g_landed{n}") for n in range(2 * GT)]
        s_cst, s_col, s_rows, s_gatew, s_keys, s_out = (
            sem(n) for n in ("cst_landed", "col_landed", "rows_landed", "gatew_landed", "keys_landed",
                             "out_stored"))
        s_stage = [sem(f"stage_stored{n}") for n in range(TB)]
        (s_zero, s_silu, s_modmm, s_mod, s_sc, s_aggr, s_sd, s_ln, s_tr, s_h, s_zmm, s_zev, s_poolmm, s_pooly,
         s_poolev, s_conv, s_gmm, s_sig, s_absl, s_expl, s_decay, s_a, s_th, s_bsq, s_sqrt, s_ix, s_gelu,
         s_lru, s_diag, s_bmm, s_bev, s_ymm, s_yres, s_x0mul, s_x0) = (
            sem(n) for n in (
                "pads_zeroed", "silu_made", "mod_summed", "mod_ready", "scales_ready", "stats_ready", "sd_ready",
                "normalised", "transposed", "h_ready", "z_summed", "z_ready", "pool_summed", "pool_input_ready",
                "pool_ready", "conv_ready", "gate_summed", "gate_ready", "abs_lambda_ready", "exp_lambda_ready",
                "decay_ready", "a_ready", "tanh_ready", "b_square_ready", "b_root_ready", "gated_x_ready",
                "gelu_ready", "lru_ready", "diag_ready", "spread_summed", "spread_ready", "y_summed", "y_read",
                "residual_scaled", "residual_ready"))
        (s_hmean, s_centre, s_qmm, s_qev, s_smm, s_sev, s_routed, s_eq, s_eqmul, s_e1e2, s_qsd,
         s_shift, s_exp, s_wt, s_imm, s_iev, s_hot, s_scmm, s_scev) = (
            sem(n) for n in (
                "head_mean_ready", "wq_centred", "q_summed", "q_ready", "scores_summed", "scores_ready",
                "scores_ranked", "match_ready", "match_times_index", "experts_ready",
                "q_sd_ready", "values_shifted", "exp_ready", "weights_ready", "index_transposed", "index_ready",
                "onehots_ready", "scattered", "scatter_staged"))
        s_amm, s_act, s_w, s_vmm, s_acc, s_zacc, s_fsd, s_fin = (
            sem(n) for n in ("expert_summed", "expert_gelu", "expert_weighted", "value_summed", "value_added",
                             "acc_zeroed", "final_sd_ready", "output_ready"))
        s_turn = sem("ranking_turn")
        s_cv, s_cl, s_cs, s_cf, s_ff = (sem(n) for n in ("vector_step", "route_step", "softmax_step",
                                                   "final_step", "final_stats"))

        src = {"ada": ada_w, "win": w_in, "wout": w_out, "wq": wq}
        at_piece = {p: n for n, p in enumerate(PIECES)}
        ada_order = [j for name, j in PIECES if name == "ada"]
        win_order = [j for name, j in PIECES if name == "win"]
        assert at_piece[("wq", 0)] % SLOTS == 0

        def piece(name, j):
            return piece_buf[:, at_piece[(name, j)] % SLOTS]

        def wait_piece(eng, name, j):
            n = at_piece[(name, j)]
            eng.wait_ge(s_piece[n % SLOTS], 16 * (n // SLOTS + 1))

        def used_up(n):
            name, j = PIECES[n]
            if name == "ada":
                return s_modmm, ada_order.index(j) + 1
            if name == "win":
                return s_zmm, 4 * (win_order.index(j) + 1)
            if name == "wout":
                return s_ymm, 2 * TB
            return s_centre, 2 * (j + 1)

        block = ctx.enter_context(nc.Block())

        @block.sync
        def _(sp):
            for tb in range(TB):
                sp.dma_start(xt[:, tb, :], x[tb * P:(tb + 1) * P, :]).then_inc(s_x[tb], 16)
            for n, (name, j) in enumerate(PIECES):
                if n >= SLOTS:
                    sp.wait_ge(*used_up(n - SLOTS))
                sp.dma_start(piece_buf[:, n % SLOTS], src[name][j]).then_inc(s_piece[n % SLOTS], 16)
            for tb in range(TB):
                sp.wait_ge(s_scev, (tb + 1) * P // 4)
                sp.dma_start(gates[:, :, tb * P:(tb + 1) * P].rearrange("i p t -> p i t"),
                             stage[tb % 2]).then_inc(s_stage[tb], 16)
            for tb in range(TB):
                sp.wait_ge(s_stage[tb], 16)

            def load_tile(s, tile):
                u_in, g_in, v_in = ut[tile], gates[tile], v[tile]
                sp.dma_start(ring_u[:, s], u_in).then_inc(s_u[s], 16)
                sp.dma_start(ring_g[:, s, :], g_in).then_inc(s_g[s], 16)
                sp.dma_start(ring_v[:, s, :], v_in).then_inc(s_v[s], 16)

            for s in range(2 * GT):
                load_tile(s, s)
            with sp.Fori(0, NT // (2 * GT) - 1) as i:
                for s in range(2 * GT):
                    tile = i * (2 * GT) + (2 * GT + s)
                    sp.wait_ge(s_amm, i * (2 * GT) + (s + 1))
                    sp.dma_start(ring_u[:, s:s + 1], ut[bass.ds(tile, 1)].rearrange("a p k n -> p a k n")
                                 ).then_inc(s_u[s], 16)
                    sp.wait_ge(s_w, i * (2 * GT) + (s + 1))
                    sp.dma_start(ring_g[:, s:s + 1, :], gates[bass.ds(tile, 1)].rearrange("a p n -> p a n")
                                 ).then_inc(s_g[s], 16)
                    if s % GT == 0:
                        sp.wait_ge(s_vmm, i * (4 * TB) + 2 * TB * (s // GT + 1))
                    sp.dma_start(ring_v[:, s:s + 1, :], v[bass.ds(tile, 1)].rearrange("a p n -> p a n")
                                 ).then_inc(s_v[s], 16)
            for tb in range(TB):
                sp.wait_ge(s_fin, tb + 1)
                sp.dma_start(out[tb * P:(tb + 1) * P, :], xt[:, tb, :]).then_inc(s_out, 16)
            sp.wait_ge(s_out, 16 * TB)

        @block.gpsimd
        def _(pool):
            def load_rows(g, b):
                for row, name in ((row_g, g), (row_b, b)):
                    r = ROWS.index(name)
                    pool.dma_start(row[:, :], rows[r:r + 1, :].to_broadcast([P, D])).then_inc(s_rows, 16)

            load_rows("ln0_g", "ln0_b")
            for buf in (zp[:, :, 0:PAD_P], pa[:, :, 0:PAD_P], pb[:, :, 0:PAD_P], zx[:, :, 0:PAD_C], wab, wxb):
                pool.memset(buf, 0.0).then_inc(s_zero, 1)
            pool.wait_ge(s_zero, 6)
            for dst, w in ((wab, wa), (wxb, wx)):
                for o in range(2):
                    pool.dma_start(dst[64 * o:64 * o + 64, :, 64 * o:64 * o + 64],
                                   w[o::2].rearrange("c i j -> i c j")).then_inc(s_gatew, 16)
            pool.dma_start(pw, pool_w.rearrange("g i j -> i g j")).then_inc(s_gatew, 16)

            def affine(nth):
                pool.wait_ge(s_tr, KD * (nth + 1))
                pool.wait_ge(s_rows, 32 * (nth + 1))
                for tb in range(TB):
                    pool.tensor_tensor(xt[:, tb, :], xt[:, tb, :], row_g[:, :], ALU.mult).then_inc(s_x0mul, 1)
                for tb in range(TB):
                    pool.wait_ge(s_x0mul, TB * nth + tb + 1)
                    pool.tensor_tensor(xt[:, tb, :], xt[:, tb, :], row_b[:, :], ALU.add).then_inc(s_x0, 1)
                pool.wait_ge(s_x0, TB * (nth + 1))

            affine(0)
            load_rows("ln1_g", "ln1_b")
            pool.wait_ge(s_sig, 8)
            for c in range(4):
                pool.tensor_tensor(gi[:, c, :], gi[:, c, :], xc[:, c, :], ALU.mult).then_inc(s_ix, 1)
            pool.wait_ge(s_ymm, 2 * TB)

            def centre(h):
                pool.wait_ge(s_hmean, h + 1)
                if h >= 2:
                    pool.wait_ge(s_qmm, 2 * (h - 1))
                pool.tensor_tensor(
                    wqc[:, h % 2], piece("wq", h // 2)[:, :, (h % 2) * DK:(h % 2 + 1) * DK],
                    hmean[:, h, :].unsqueeze(2).to_broadcast([P, KD, DK]), ALU.add).then_inc(s_centre, 1)

            pool.dma_start(keys[:, 0, :], k1t).then_inc(s_keys, 16)
            pool.dma_start(keys[:, 1, :], k2t).then_inc(s_keys, 16)
            centre(0)
            centre(1)
            affine(1)
            load_rows("ln2_g", "ln2_b")
            for h in range(H):
                if h + 2 < H:
                    centre(h + 2)
                pool.wait_ge(s_eq, h + 1)
                eb = eq_b.rearrange("p (t j) a -> p t j a", t=TB)
                pool.tensor_tensor(eb, eb, s_posf[:, 1].unsqueeze(2).to_broadcast([P, TB, K, K]),
                                   ALU.mult).then_inc(s_eqmul, 1)
            for tb in range(0, TB, 2):
                pool.wait_ge(s_stage[tb], 16)
            pool.memset(acc, 0.0).then_inc(s_zacc, 1)

        @block.scalar
        def _(act):
            act.dma_start(col[:, :], cols).then_inc(s_col, 16)
            act.dma_start(cst[:, :], consts).then_inc(s_cst, 16)
            act.wait_ge(s_col, 16)
            act.wait_ge(s_cst, 16)
            act.activation(silu_c, vec("c"), ACT.Silu).then_inc(s_silu, 1)
            act.wait_ge(s_absl, 1)
            act.activation(t4[2], t4[0], ACT.Exp, scale=-1.0).then_inc(s_expl, 1)

            def root_of_variance(nth):
                act.wait_ge(s_aggr, nth + 1)
                act.activation(sd[:, :], mv[:, :, 1], ACT.Sqrt, bias=eps).then_inc(s_sd, 1)

            def modulate(nth, banks, scale, bias):
                act.wait_ge(s_sc, nth + 1)
                for k in range(KD):
                    act.wait_ge(s_tr, KD * nth + k + 1)
                    act.activation(hT[:, k, :], bank[banks[k % len(banks)]][:, :], ACT.Identity,
                                   bias=bias[:, k:k + 1], scale=scale[:, k:k + 1]).then_inc(s_h, 1)

            def spread(nth):
                for b in range(2):
                    act.wait_ge(s_bmm, 2 * nth + b + 1)
                    act.activation(row_gate[:, b * 512:(b + 1) * 512], bank[2 + b][:, :], ACT.Copy
                                   ).then_inc(s_bev, 1)

            root_of_variance(0)
            modulate(0, (2, 3, 4, 5), scale1, bias1)
            act.wait_ge(s_zero, 4)
            for n in range(12):
                dst = (zx[:, n % 4, PAD_C:], zp[:, n % 4, PAD_P:], zg[:, n % 4, :])[n // 4]
                act.wait_ge(s_zmm, n + 1)
                act.activation(dst, bank[n % 2][:, :], ACT.Copy).then_inc(s_zev, 1)
            act.wait_ge(s_zev, 12)
            for c in range(4):
                act.activation(zg[:, c, :], zg[:, c, :], ACT.Gelu_apprx_tanh).then_inc(s_gelu, 1)
            for n in range(8):
                c, dst, bias = n // 2, (gr, gi)[n % 2], ("lru_ba", "lru_bx")[n % 2]
                act.wait_ge(s_gmm, n + 1)
                act.activation(dst[:, c, :], bank[4 + n % 2][:, :], ACT.Sigmoid, bias=vec(bias, c)).then_inc(s_sig, 1)
            for g in range(NG):
                act.wait_ge(s_poolmm, g + 1)
                act.activation(yT[:, g, :], bank[(6, 0)[g % 2]][:, :], ACT.Copy, scale=vec("pool_scale", g)
                               ).then_inc(s_poolev, 1)
            act.wait_ge(s_decay, 1)
            act.wait_ge(s_sig, 8)
            for c in range(4):
                act.activation(pa[:, c, PAD_P:], gr[:, c, :], ACT.Exp, scale=decay[:, c:c + 1]).then_inc(s_a, 1)
            act.wait_ge(s_a, 4)
            for c in range(4):
                act.activation(gr[:, c, :], gr[:, c, :], ACT.Tanh, scale=ndecay[:, c:c + 1]).then_inc(s_th, 1)
            spread(0)
            for c in range(4):
                act.wait_ge(s_bsq, c + 1)
                act.activation(pb[:, c, PAD_P:], pb[:, c, PAD_P:], ACT.Sqrt).then_inc(s_sqrt, 1)
            root_of_variance(1)
            modulate(1, (4, 5), scale2, bias2)

            def queries(i, par, h, first):
                if not first:
                    act.wait_ge(s_smm, h - 1)
                for half in range(2):
                    act.wait_ge(s_qmm, h * 2 + (half + 1))
                    act.activation(qT[:, par, half, :], bank[half][:, :], ACT.Copy)
                    act.activation(sq[:, par, half, :], bank[half][:, :], ACT.Square).then_inc(s_qev, 1)

            def scores(par, h, first):
                act.wait_ge(s_smm, h + 1)
                if not first:
                    act.wait_ge(s_routed, h - 1)
                for b in range(2):
                    act.activation(s_all[:, par, 2 * b:2 * b + 2, :],
                                   bank[(2, 5)[par] + b][:, :].rearrange("p (t n) -> p t n", t=2), ACT.Copy
                                   ).then_inc(s_sev, 1)

            queries(0, 0, 0, True)
            queries(0, 1, 1, True)
            scores(0, 0, True)
            queries(1, 0, 2, False)
            scores(1, 1, True)
            with act.Fori(1, H // 2 - 1) as i:
                queries(i, 1, i * 2 + 1, False)
                scores(0, i * 2, False)
                queries(i, 0, i * 2 + 2, False)
                scores(1, i * 2 + 1, False)
            queries(3, 1, H - 1, False)
            scores(0, H - 2, False)
            scores(1, H - 1, False)
            act.activation(pk[:, 0, :], bank[4][:, 0:TB * H], ACT.Sqrt, bias=eps).then_inc(s_qsd, 1)
            act.wait_ge(s_shift, 1)
            act.activation(vs, wt, ACT.Exp).then_inc(s_exp, 1)
            for n, dst in enumerate((i1T, i2T, wT)):
                act.wait_ge(s_imm, n + 1)
                act.activation(dst, bank[n][:, :], ACT.Copy).then_inc(s_iev, 1)
            spread(1)
            for tb in range(TB):
                if tb >= 2:
                    act.wait_ge(s_stage[tb - 2], 16)
                with act.Fori(0, P // TOK) as i:
                    for q in range(TOK // 4):
                        act.wait_ge(s_scmm, i * (TOK // 4) + (tb * P // 4 + q + 1))
                        dst = stage[tb % 2][:, :, bass.ds(i * TOK + 4 * q, 4)].rearrange("p i t -> p t i")
                        act.activation(dst, bank[q][:, :].rearrange("p (t i) -> p t i", t=4), ACT.Copy
                                       ).then_inc(s_scev, 1)

            def gelu(j, n, first):
                act.wait_ge(s_amm, n + 1)
                if not first:
                    act.wait_ge(s_w, n - (GT - 1))
                act.activation(ring_a[:, j, :], bank[j][:, :], ACT.Gelu_apprx_tanh).then_inc(s_act, 1)

            for tb in range(0, TB, 2):
                act.wait_ge(s_stage[tb], 16)
            for j in range(GT):
                gelu(j, j, True)
            with act.Fori(1, NT // GT) as i:
                for j in range(GT):
                    gelu(j, i * GT + j, False)
            for tb in range(TB):
                act.wait_ge(s_ff, tb + 1)
                act.activation(sd[:, tb:tb + 1], mv[:, tb, 1:2], ACT.Sqrt, bias=eps).then_inc(s_fsd, 1)

        @block.tensor
        def _(pe):
            def modulation(j):
                wait_piece(pe, "ada", j)
                for m in range(4):
                    for k in range(KD):
                        mm = pe.matmul(bank[7][:, 4 * j + m:4 * j + m + 1], piece("ada", j)[:, k, m * P:(m + 1) * P],
                                       silu_c[:, k:k + 1], start=(k == 0), stop=(k == KD - 1))
                mm.then_inc(s_modmm, 1)

            def transposes(nth, banks):
                pe.wait_ge(s_ln, TB * (nth + 1))
                for k in range(KD):
                    if k >= len(banks):
                        pe.wait_ge(s_h, KD * nth + k - len(banks) + 1)
                    for tb in range(TB):
                        mm = pe.transpose(bank[banks[k % len(banks)]][:, tb * P:(tb + 1) * P],
                                          xt[:, tb, k * P:(k + 1) * P], ident)
                    mm.then_inc(s_tr, 1)

            def spread(nth):
                for b in range(2):
                    for k in range(4 * b, 4 * b + 4):
                        pe.wait_ge(s_diag, KD * nth + k + 1)
                        mm = pe.matmul(bank[2 + b][:, (k % 4) * P:(k % 4 + 1) * P], ones, diag[:, k, :],
                                       start=True, stop=True)
                    mm.then_inc(s_bmm, 1)

            pe.wait_ge(s_silu, 1)
            for j in range(4):
                modulation(j)
            pe.wait_ge(s_cst, 16)
            transposes(0, (2, 3, 4, 5))
            pe.wait_ge(s_h, KD)
            for n in range(12):
                wait_piece(pe, "win", win_order[n // 4])
                if n >= 2:
                    pe.wait_ge(s_zev, n - 1)
                for k in range(KD):
                    mm = pe.matmul(bank[n % 2][:, :], piece("win", win_order[n // 4])[:, k, (n % 4) * P:(n % 4 + 1) * P],
                                   hT[:, k, :], start=(k == 0), stop=(k == KD - 1))
                mm.then_inc(s_zmm, 1)
            modulation(4)
            modulation(5)
            pe.wait_ge(s_gatew, 80)
            for n in range(8):
                c = n // 2
                pe.wait_ge(s_conv, c + 1)
                if n >= 2:
                    pe.wait_ge(s_sig, n - 1)
                pe.matmul(bank[4 + n % 2][:, :], (wab, wxb)[n % 2][:, c, :], xc[:, c, :], start=True, stop=True
                          ).then_inc(s_gmm, 1)
            pe.wait_ge(s_zev, 12)
            for g in range(NG):
                pe.wait_ge(s_pooly, g + 1)
                if g >= 2:
                    pe.wait_ge(s_poolev, g - 1)
                pe.matmul(bank[(6, 0)[g % 2]][:, :], pw[:, g, :], (pa, pb)[g % 2][:, g, PAD_P:],
                          start=True, stop=True).then_inc(s_poolmm, 1)
            spread(0)
            for j in range(6, 11):
                modulation(j)
            pe.wait_ge(s_poolev, NG)
            pe.wait_ge(s_bev, 2)
            pe.wait_ge(s_lru, 4)
            wait_piece(pe, "wout", 0)
            wait_piece(pe, "wout", 1)
            for n in range(2 * TB):
                if n >= 4:
                    pe.wait_ge(s_yres, n - 3)
                for k in range(KD):
                    mm = pe.matmul(bank[n % 4][:, :], yT[:, k, (n // 2) * P:(n // 2 + 1) * P],
                                   piece("wout", n % 2)[:, k, :], start=(k == 0), stop=(k == KD - 1))
                mm.then_inc(s_ymm, 1)
            transposes(1, (4, 5))

            def queries(par, h, first):
                pe.wait_ge(s_centre, h + 1)
                for half in range(2):
                    if not first:
                        pe.wait_ge(s_qev, h * 2 + (half - 1))
                    for k in range(KD):
                        mm = pe.matmul(bank[half][:, :], wqc[:, par, k, half * P:(half + 1) * P], hT[:, k, :],
                                       start=(k == 0), stop=(k == KD - 1))
                    mm.then_inc(s_qmm, 1)

            def scores(par, h, first, var_at):
                pe.wait_ge(s_qev, h * 2 + 2)
                if not first:
                    pe.wait_ge(s_sev, h * 2 - 2)
                for tb in range(TB):
                    for half in range(2):
                        at = (tb % 2) * DK + half * NK
                        pe.matmul(bank[(2, 5)[par] + tb // 2][:, at:at + NK],
                                  qT[:, par, half, tb * P:(tb + 1) * P], keys[:, half, :], start=True, stop=True)
                for tb in range(TB):
                    for half in range(2):
                        mm = pe.matmul(bank[4][:, var_at(tb)], sq[:, par, half, tb * P:(tb + 1) * P], mean_col,
                                       start=(half == 0), stop=(half == 1))
                mm.then_inc(s_smm, 1)

            def static_at(h):
                return lambda tb: slice(h * TB + tb, h * TB + tb + 1)

            def register_at(h):
                return lambda tb: bass.ds(h * TB + tb, 1)

            pe.wait_ge(s_h, 2 * KD)
            pe.wait_ge(s_yres, 2 * TB)
            queries(0, 0, True)
            queries(1, 1, False)
            pe.wait_ge(s_keys, 32)
            scores(0, 0, True, static_at(0))
            queries(0, 2, False)
            scores(1, 1, True, static_at(1))
            for i in range(1, H // 2 - 1):
                queries(1, i * 2 + 1, False)
                scores(0, i * 2, False, static_at(i * 2))
                queries(0, i * 2 + 2, False)
                scores(1, i * 2 + 1, False, static_at(i * 2 + 1))
            queries(1, H - 1, False)
            scores(0, H - 2, False, static_at(H - 2))
            scores(1, H - 1, False, static_at(H - 1))
            modulation(11)
            pe.wait_ge(s_qev, 2 * H)
            pe.wait_ge(s_sev, 2 * H)
            pe.wait_ge(s_wt, 1)
            pe.wait_ge(s_e1e2, H)
            for n, m in enumerate((e1, e2, wt)):
                for tb in range(TB):
                    mm = pe.transpose(bank[n][:, tb * P:(tb + 1) * P], m[:, tb, :], ident)
                mm.then_inc(s_imm, 1)
            pe.wait_ge(s_iev, 3)
            spread(1)
            pe.wait_ge(s_bev, 4)

            def scatter(i, first):
                for q in range(TOK // 4):
                    pe.wait_ge(s_hot, i * (TOK // 4) + (q + 1))
                    if not first:
                        pe.wait_ge(s_scev, i * (TOK // 4) + (q + 1 - TOK // 4))
                    for t in range(4):
                        mm = pe.matmul(bank[q][:, t * P:(t + 1) * P], onehot[:, 4 * q + t, :],
                                       onehot_w[:, 4 * q + t, :], start=True, stop=True)
                    mm.then_inc(s_scmm, 1)

            scatter(0, True)
            with pe.Fori(1, S // TOK) as i:
                scatter(i, False)

            def expert_inputs(j, s, landed, n, first):
                pe.wait_ge(s_u[s], landed)
                if not first:
                    pe.wait_ge(s_act, n - (GT - 1))
                for k in range(KD):
                    mm = pe.matmul(bank[j][:, :], ring_u[:, s, k, :], hT[:, k, :],
                                   start=(k == 0), stop=(k == KD - 1))
                mm.then_inc(s_amm, 1)

            def values(g2, o, n, first):
                tb, half = o // 2, o % 2
                if not first:
                    pe.wait_ge(s_acc, n - 3)
                for j in range(GT):
                    s = GT * g2 + j
                    mm = pe.matmul(bank[4 + o % 4][:, :], ring_w[:, s, tb * P:(tb + 1) * P],
                                   ring_v[:, s, half * 512:(half + 1) * 512], start=(j == 0), stop=(j == GT - 1))
                mm.then_inc(s_vmm, 1)

            def group(i, g2, first, last):
                g = i * 2 + g2
                pe.wait_ge(s_w, g * GT + GT)
                for j in range(GT):
                    pe.wait_ge(s_v[GT * g2 + j], i * 16 + 16)
                for j in range(GT):
                    if not last:
                        expert_inputs(j, GT * (1 - g2) + j, (i + g2) * 16 + 16, g * GT + (GT + j), False)
                    for o in (2 * j, 2 * j + 1):
                        values(g2, o, g * (2 * TB) + o, first and o < 4)

            pe.wait_ge(s_scev, S // 4)
            for j in range(GT):
                expert_inputs(j, j, 16, j, True)
            group(0, 0, True, False)
            group(0, 1, False, False)
            with pe.Fori(1, NT // (2 * GT) - 1) as i:
                group(i, 0, False, False)
                group(i, 1, False, False)
            group(NT // (2 * GT) - 1, 0, False, False)
            group(NT // (2 * GT) - 1, 1, False, True)

        @block.vector
        def _(ve):
            steps = Chain(ve, s_cv)
            link = steps.link

            def stats_and_normalise(nth):
                for tb in range(TB):
                    if nth == 0:
                        ve.wait_ge(s_x[tb], 16)
                    for b in range(2):
                        last = ve.bn_stats(st[:, tb, b, :], xt[:, tb, b * 512:(b + 1) * 512])
                link(last)
                for tb in range(TB):
                    last = ve.bn_aggr(mv[:, tb, :], st[:, tb, :, :])
                last.then_inc(s_aggr, 1)
                ve.wait_ge(s_sd, nth + 1)
                link(ve.reciprocal(rstd[:, :], sd[:, :]))
                ve.wait_ge(s_aggr, nth + 1)
                for tb in range(TB):
                    ve.tensor_scalar(xt[:, tb, :], xt[:, tb, :], mv[:, tb, 0:1], rstd[:, tb:tb + 1],
                                     ALU.subtract, ALU.mult).then_inc(s_ln, 1)

            def read_mod(a, b, pieces):
                ve.wait_ge(s_modmm, pieces)
                o = COLS["ada_b"][0]
                link(ve.tensor_tensor(mod[:, a:b], bank[7][:, a:b], col[:, o + a:o + b], ALU.add))

            def scales(shift, scale, g, b, out_scale, out_bias):
                ve.scalar_tensor_tensor(out=out_scale, in0=mod[:, scale:scale + 8], scalar=1.0, in1=vec(g),
                                        op0=ALU.add, op1=ALU.mult)
                link(ve.scalar_tensor_tensor(out=out_bias, in0=mod[:, scale:scale + 8], scalar=1.0, in1=vec(b),
                                             op0=ALU.add, op1=ALU.mult))
                ve.tensor_tensor(out_bias, out_bias, mod[:, shift:shift + 8], ALU.add).then_inc(s_sc, 1)

            def gate_diag(a):
                for k in range(KD):
                    ve.tensor_scalar(diag[:, k, :], ident, mod[:, a + k:a + k + 1], None, ALU.mult
                                     ).then_inc(s_diag, 1)

            ve.wait_ge(s_col, 16)
            lam, (al, m, e, r, z, z2, p) = vec("lam"), t4
            ve.tensor_scalar(m, lam, -1.0, 0.0, ALU.mult, ALU.max)
            ve.scalar_tensor_tensor(out=al, in0=lam, scalar=-1.0, in1=lam, op0=ALU.mult, op1=ALU.max
                                    ).then_inc(s_absl, 1)
            stats_and_normalise(0)
            ve.wait_ge(s_expl, 1)
            link(ve.tensor_scalar(z, e, 2.0, None, ALU.add))
            link(ve.reciprocal(r, z))
            link(ve.tensor_tensor(z, e, r, ALU.mult))
            link(ve.tensor_tensor(z2, z, z, ALU.mult))
            link(ve.tensor_scalar(p, z2, 1.0 / 19, None, ALU.mult))
            for n in range(17, 1, -2):
                link(ve.scalar_tensor_tensor(out=p, in0=p, scalar=1.0 / n, in1=z2, op0=ALU.add, op1=ALU.mult))
            link(ve.scalar_tensor_tensor(out=p, in0=p, scalar=1.0, in1=z, op0=ALU.add, op1=ALU.mult))
            link(ve.scalar_tensor_tensor(out=p, in0=p, scalar=2.0, in1=m, op0=ALU.mult, op1=ALU.add))
            ve.tensor_scalar(decay, p, -LRU_C, None, ALU.mult)
            ve.tensor_scalar(ndecay, p, LRU_C, None, ALU.mult).then_inc(s_decay, 1)

            read_mod(0, 16, 4)
            scales(0, 8, "ln0_g", "ln0_b", scale1, bias1)

            ve.wait_ge(s_zero, 6)
            for t in range(CONV_W):
                for c in range(4):
                    w = vec("conv_w", 4 * t + c)
                    shifted = zx[:, c, PAD_C - CONV_W + 1 + t:PAD_C - CONV_W + 1 + t + S]
                    if t == 0:
                        ve.wait_ge(s_zev, c + 1)
                        last = ve.tensor_scalar(xc[:, c, :], shifted, w, vec("conv_b", c), ALU.mult, ALU.add)
                    else:
                        last = ve.scalar_tensor_tensor(out=xc[:, c, :], in0=shifted, scalar=w, in1=xc[:, c, :],
                                                       op0=ALU.mult, op1=ALU.add)
                    if t == CONV_W - 1:
                        last.then_inc(s_conv, 1)
                if t < CONV_W - 1:
                    link(last)
            ve.wait_ge(s_zev, 8)
            bufs = (zp, pa, pb, pa, pb)
            for n, w in enumerate(WINDOWS):
                a, b = bufs[n], bufs[n + 1]
                link(ve.tensor_tensor(b[:, n:, PAD_P:], a[:, n:, PAD_P:], a[:, n:, PAD_P - w // 2:PAD_P - w // 2 + S],
                                      ALU.add))
            for g, w in enumerate(WINDOWS):
                last = ve.tensor_tensor(ramp[:, g, :], bufs[g + 1][:, g, PAD_P:2 * PAD_P], inv_count[:, g, :], ALU.mult)
            link(last)
            for g, w in enumerate(WINDOWS):
                b = bufs[g + 1][:, g, PAD_P:]
                last = ve.scalar_tensor_tensor(out=b, in0=b, scalar=1.0 / w, in1=zp[:, g, PAD_P:],
                                               op0=ALU.mult, op1=ALU.subtract)
            link(last)
            for g in range(NG):
                ve.tensor_tensor(bufs[g + 1][:, g, PAD_P:2 * PAD_P], ramp[:, g, :], zp[:, g, PAD_P:2 * PAD_P],
                                 ALU.subtract).then_inc(s_pooly, 1)
            read_mod(16, 24, 6)
            gate_diag(16)
            ve.wait_ge(s_poolmm, NG)
            for c in range(4):
                ve.wait_ge(s_a, c + 1)
                last = ve.tensor_tensor(pb[:, c, PAD_P:], pa[:, c, PAD_P:], pa[:, c, PAD_P:], ALU.mult)
            link(last)
            for c in range(4):
                ve.wait_ge(s_th, c + 1)
                ve.scalar_tensor_tensor(out=pb[:, c, PAD_P:], in0=pb[:, c, PAD_P:], scalar=1.0, in1=gr[:, c, :],
                                        op0=ALU.add, op1=ALU.mult).then_inc(s_bsq, 1)
            for c in range(4):
                ve.wait_ge(s_sqrt, c + 1)
                ve.wait_ge(s_ix, c + 1)
                last = ve.tensor_tensor(pb[:, c, PAD_P:], pb[:, c, PAD_P:], gi[:, c, :], ALU.mult)
            link(last)
            ve.wait_ge(s_ix, 4)
            for c in range(4):
                last = ve.tensor_tensor_scan(xc[:, c, :], pa[:, c, PAD_P:], pb[:, c, PAD_P:], 0.0, ALU.mult, ALU.add)
            link(last)
            ve.wait_ge(s_gelu, 4)
            for c in range(4):
                ve.tensor_tensor(yT[:, NG + c, :], xc[:, c, :], zg[:, c, :], ALU.mult).then_inc(s_lru, 1)
            read_mod(24, 44, 11)
            scales(24, 32, "ln1_g", "ln1_b", scale2, bias2)
            ve.wait_ge(s_bev, 2)
            ve.wait_ge(s_x0, TB)
            ve.wait_ge(s_lru, 4)
            for tb in range(TB):
                for half in range(2):
                    n = 2 * tb + half
                    ve.wait_ge(s_ymm, n + 1)
                    ve.tensor_tensor(zg[:, n % 4, :], bank[n % 4][:, :], row_gate[:, half * 512:(half + 1) * 512],
                                     ALU.mult).then_inc(s_yres, 1)
                ve.wait_ge(s_yres, 2 * tb + 2)
                for half in range(2):
                    part = xt[:, tb, half * 512:(half + 1) * 512]
                    last = ve.scalar_tensor_tensor(out=part, in0=part, scalar=ALPHA, in1=zg[:, (2 * tb + half) % 4, :],
                                                   op0=ALU.mult, op1=ALU.add)
            link(last)
            stats_and_normalise(1)

            def head_means(i):
                for par in range(2):
                    w = piece_buf[:, bass.ds(i, 1), :, par * DK:(par + 1) * DK]
                    last = ve.tensor_reduce(hsum[:, bass.ds(i * 2 + par, 1), :], w, AX.X, ALU.add)
                return last

            def scaled_means(i):
                last = ve.tensor_scalar(hmean[:, bass.ds(i * 2, 1), :], hsum[:, bass.ds(i * 2, 1), :],
                                        -1.0 / DK, None, ALU.mult).then_inc(s_hmean, 1)
                ve.tensor_scalar(hmean[:, bass.ds(i * 2 + 1, 1), :], hsum[:, bass.ds(i * 2 + 1, 1), :],
                                 -1.0 / DK, None, ALU.mult).then_inc(s_hmean, 1)

            def top_k(parts, step, done=None):
                for val, idx, data in parts:
                    last = ve.max(val[:, 0:8], data)
                step(last)
                for val, idx, data in parts:
                    ve.max_index(idx[:, 0:8], val[:, 0:8], data)
                for val, idx, data in parts:
                    last = ve.match_replace(data, val[:, 0:8], data, DROPPED)
                step(last)
                for val, idx, data in parts:
                    last = ve.max(val[:, 8:16], data)
                step(last)
                for val, idx, data in parts:
                    last = ve.max_index(idx[:, 8:16], val[:, 8:16], data)
                return last

            ci = c_idx.rearrange("p t k -> p (t k)").bitcast(U32)
            dci = [dec[:, n, :].bitcast(U32) for n in range(4)]
            ka, kb, low = dec[:, 4, :], dec[:, 5, :], dec[:, 6, :]
            iota16 = iota[:, 0:K].unsqueeze(1).to_broadcast([P, TB * K, K])

            def route(par, h, chain):
                def step(ins):
                    chain.link(ins)
                    ve.sem_inc(s_turn, 1)

                ve.wait_ge(s_sev, h * 2 + 2)
                ve.sem_inc(s_turn, 1)
                last = top_k([(s_val[:, half, tb, :], s_pos[:, half, tb, :].bitcast(U32),
                               s_all[:, par, tb, half * NK:(half + 1) * NK])
                              for tb in range(TB) for half in range(2)], step)
                last.then_inc(s_routed, 1)
                ve.wait_ge(s_routed, h + 1)
                ve.tensor_copy(s_posf, s_pos.bitcast(U32))
                ve.tensor_tensor(cand[:, :, 0:CAND_A].rearrange("p t (a b) -> p t a b", a=4),
                                 s_val[:, 0, :, 0:4].unsqueeze(3).to_broadcast([P, TB, 4, K]),
                                 s_val[:, 1, :, :].unsqueeze(2).to_broadcast([P, TB, 4, K]), ALU.add)
                step(ve.tensor_tensor(cand[:, :, CAND_A:].rearrange("p t (a b) -> p t a b", a=K - 4),
                                      s_val[:, 0, :, 4:].unsqueeze(3).to_broadcast([P, TB, K - 4, 4]),
                                      s_val[:, 1, :, 0:4].unsqueeze(2).to_broadcast([P, TB, K - 4, 4]), ALU.add))
                step(top_k([(c_val[:, tb, :], c_idx[:, tb, :].bitcast(U32), cand[:, tb, :]) for tb in range(TB)], step))
                ve.tensor_copy(vs[:, :, bass.ds(h * K, K)], c_val)
                ve.tensor_scalar(dci[0], ci, 2, None, ALU.logical_shift_right)
                ve.tensor_scalar(dci[1], ci, 4, None, ALU.logical_shift_right)
                ve.tensor_scalar(dci[2], ci, 12, None, ALU.bitwise_and)
                step(ve.tensor_scalar(dci[3], ci, 3, None, ALU.bitwise_and))
                ve.scalar_tensor_tensor(out=ka, in0=dci[0], scalar=-12.0, in1=dci[1], op0=ALU.add, op1=ALU.max)
                step(ve.scalar_tensor_tensor(out=low, in0=ci, scalar=float(CAND_A), in1=dci[2],
                                             op0=ALU.is_lt, op1=ALU.mult))
                step(ve.tensor_tensor(kb, low, dci[3], ALU.add))
                ve.tensor_tensor(eq_b, kb.unsqueeze(2).to_broadcast([P, TB * K, K]), iota16, ALU.is_equal
                                 ).then_inc(s_eq, 1)
                step(ve.tensor_tensor(eq_a, ka.unsqueeze(2).to_broadcast([P, TB * K, K]), iota16, ALU.is_equal))
                ea = eq_a.rearrange("p (t j) a -> p t j a", t=TB)
                eb = eq_b.rearrange("p (t j) a -> p t j a", t=TB)
                step(ve.tensor_tensor(ea, ea, s_posf[:, 0].unsqueeze(2).to_broadcast([P, TB, K, K]), ALU.mult))
                ve.tensor_reduce(e1[:, :, bass.ds(h * K, K)], ea, AX.X, ALU.add)
                ve.wait_ge(s_eqmul, h + 1)
                ve.tensor_reduce(e2[:, :, bass.ds(h * K, K)], eb, AX.X, ALU.add).then_inc(s_e1e2, 1)

            for j in range(4):
                wait_piece(ve, "wq", j)
            link(head_means(0))
            scaled_means(0)
            per = 1 + 2 * STEPS_ROUTE
            with ve.Fori(0, H // 2 - 1) as i:
                chain = Chain(ve, s_cl, i, per)
                chain.link(head_means(i + 1))
                scaled_means(i + 1)
                route(0, i * 2, chain)
                route(1, i * 2 + 1, chain)
                assert chain.n == per, chain.n
            chain = Chain(ve, s_cl)
            chain.n = (H // 2 - 1) * per
            route(0, H - 2, chain)
            route(1, H - 1, chain)

            link = Chain(ve, s_cs).link
            ve.wait_ge(s_qsd, 1)
            link(ve.reciprocal(pk[:, 1, :], pk[:, 0, :]))
            v4 = vs.rearrange("p t (h k) -> p t h k", h=H)
            w4 = wt.rearrange("p t (h k) -> p t h k", h=H)
            full = [P, TB, H, K]
            link(ve.tensor_tensor(v4, v4, pk[:, 1, :].rearrange("p (h t) -> p t h", h=H).unsqueeze(3).to_broadcast(full),
                                  ALU.mult))
            ve.tensor_tensor(w4, v4, v4[:, :, :, 0:1].to_broadcast(full), ALU.subtract).then_inc(s_shift, 1)
            ve.wait_ge(s_exp, 1)
            link(ve.tensor_reduce(pk[:, 2, :].rearrange("p (t h) -> p t h", t=TB), v4, AX.X, ALU.add))
            link(ve.reciprocal(pk[:, 3, :], pk[:, 2, :]))
            ve.tensor_tensor(w4, v4, pk[:, 3, :].rearrange("p (t h) -> p t h", t=TB).unsqueeze(3).to_broadcast(full),
                             ALU.mult).then_inc(s_wt, 1)
            link = steps.link
            read_mod(44, 48, 12)
            gate_diag(40)

            def onehots(i, first):
                for q in range(TOK // 4):
                    if not first:
                        ve.wait_ge(s_scmm, i * (TOK // 4) + (q + 1 - TOK // 4))
                    for s in range(4 * q, 4 * q + 4):
                        t = bass.ds(i * TOK + s, 1)
                        ve.tensor_scalar(onehot_w[:, s, :], iota, i1T[:, t], wT[:, t], ALU.is_equal, ALU.mult)
                        last = ve.tensor_scalar(onehot[:, s, :], iota, i2T[:, t], None, ALU.is_equal)
                    last.then_inc(s_hot, 1)

            ve.wait_ge(s_iev, 3)
            onehots(0, True)
            with ve.Fori(1, S // TOK) as i:
                onehots(i, False)

            def weigh(j, s, landed, n, free):
                ve.wait_ge(s_act, n + 1)
                ve.wait_ge(s_g[s], landed)
                if free is not None:
                    ve.wait_ge(s_vmm, free)
                ve.tensor_tensor(ring_w[:, s, :], ring_a[:, j, :], ring_g[:, s, :], ALU.mult).then_inc(s_w, 1)

            def add_up(o, n):
                ve.wait_ge(s_vmm, n + 1)
                part = acc[:, o // 2, (o % 2) * 512:(o % 2 + 1) * 512]
                ve.tensor_tensor(part, part, bank[4 + o % 4][:, :], ALU.add).then_inc(s_acc, 1)

            def group(i, g2, first, last):
                g = i * 2 + g2
                if not first:
                    ve.wait_ge(s_acc, g * (2 * TB))
                for j in range(GT):
                    if not last:
                        weigh(j, GT * (1 - g2) + j, (i + g2) * 16 + 16, g * GT + (GT + j),
                              None if first else g * (2 * TB))
                    for o in (2 * j, 2 * j + 1):
                        add_up(o, g * (2 * TB) + o)

            ve.wait_ge(s_zacc, 1)
            for j in range(GT):
                weigh(j, j, 16, j, None)
            group(0, 0, True, False)
            group(0, 1, False, False)
            with ve.Fori(1, NT // (2 * GT) - 1) as i:
                group(i, 0, False, False)
                group(i, 1, False, False)
            group(NT // (2 * GT) - 1, 0, False, False)
            group(NT // (2 * GT) - 1, 1, False, True)

            ve.wait_ge(s_acc, NT // GT * 2 * TB)
            ve.wait_ge(s_bev, 4)
            ve.wait_ge(s_x0, 2 * TB)
            ve.wait_ge(s_rows, 96)
            link = Chain(ve, s_cf).link
            for tb in range(TB):
                link(ve.tensor_tensor(tmp, acc[:, tb, :], row_gate[:, :], ALU.mult))
                link(ve.scalar_tensor_tensor(out=xt[:, tb, :], in0=xt[:, tb, :], scalar=ALPHA, in1=tmp,
                                             op0=ALU.mult, op1=ALU.add))
                for b in range(2):
                    last = ve.bn_stats(st[:, tb, b, :], xt[:, tb, b * 512:(b + 1) * 512])
                link(last)
                ve.bn_aggr(mv[:, tb, :], st[:, tb, :, :]).then_inc(s_ff, 1)
            for tb in range(TB):
                ve.wait_ge(s_fsd, tb + 1)
                link(ve.reciprocal(rstd[:, tb:tb + 1], sd[:, tb:tb + 1]))
                link(ve.tensor_scalar(xt[:, tb, :], xt[:, tb, :], mv[:, tb, 0:1], rstd[:, tb:tb + 1],
                                      ALU.subtract, ALU.mult))
                link(ve.tensor_tensor(xt[:, tb, :], xt[:, tb, :], row_g[:, :], ALU.mult))
                ve.tensor_tensor(xt[:, tb, :], xt[:, tb, :], row_b[:, :], ALU.add).then_inc(s_fin, 1)


STEPS_ROUTE = 13


def constants():
    import numpy as np

    a = np.zeros((P, NCONST), np.float32)
    a[:, C_ID:C_ID + P] = np.eye(P)
    a[:, C_IOTA:C_IOTA + P] = np.arange(P)
    a[:, C_ONE:C_ONE + P] = 1.0
    a[:, C_MEAN] = 1.0 / DK
    a[:, C_EPS] = LN_EPS
    for g, w in enumerate(WINDOWS):
        for t in range(PAD_P):
            a[:, C_CNT + g * PAD_P + t] = 1.0 / min(t + 1, w)
    return a


def kernel(x, c, ln0_g, ln0_b, ada_w, ada_b, w_in, pool_w, pool_scale, conv_w, conv_b,
           lru_wa, lru_ba, lru_wx, lru_bx, lru_lambda, w_out, ln1_g, ln1_b,
           peer_wq, peer_k1, peer_k2, peer_u, peer_v, ln2_g, ln2_b):
    import numpy as np
    import concourse.bacc as bacc
    from concourse.bass_utils import run_bass_kernel_spmd

    def chunks(a):
        return np.asarray(a).reshape(-1, P).T

    def pieces(w):
        w = np.asarray(w).reshape(KD, P, -1, CHUNK_C)
        return np.ascontiguousarray(w.transpose(2, 1, 0, 3))

    cols = np.concatenate([chunks(a) for a in (
        c, ada_b, ln0_g, ln0_b, ln1_g, ln1_b, pool_scale, conv_b, lru_ba, lru_bx, lru_lambda, conv_w)], axis=1)
    rows = np.stack([np.asarray(a).reshape(D) for a in (ln0_g, ln0_b, ln1_g, ln1_b, ln2_g, ln2_b)])
    arrays = {
        "x": np.asarray(x)[0], "cols": cols, "rows": rows, "consts": constants(),
        "ada_w": pieces(ada_w), "w_in": pieces(w_in), "w_out": pieces(w_out), "wq": pieces(peer_wq),
        "pool_w": np.asarray(pool_w)[0], "wa": np.asarray(lru_wa)[0], "wx": np.asarray(lru_wx)[0],
        "k1t": np.asarray(peer_k1)[0].T, "k2t": np.asarray(peer_k2)[0].T,
        "ut": np.asarray(peer_u)[0].reshape(NT, P, KD, P).transpose(0, 3, 2, 1),
        "v": np.asarray(peer_v)[0].reshape(NT, P, D),
    }
    arrays = {n: np.ascontiguousarray(a) for n, a in arrays.items()}
    nc = bacc.Bacc("TRN2", target_bir_lowering=False, num_devices=1)
    ins = {n: nc.dram_tensor(n + "_dram", a.shape, F32, kind="ExternalInput").ap() for n, a in arrays.items()}
    out = nc.dram_tensor("out_dram", (S, D), F32, kind="ExternalOutput").ap()
    build(nc, *(ins[n] for n in ("x", "cols", "rows", "consts", "ada_w", "w_in", "w_out", "wq", "pool_w",
                                 "wa", "wx", "k1t", "k2t", "ut", "v")), out)
    r = run_bass_kernel_spmd(nc, [{n + "_dram": a for n, a in arrays.items()}], core_ids=[0])
    return r.results[0]["out_dram"].reshape(1, S, D)
```

```python
from contextlib import ExitStack

import concourse.bass as bass
from concourse import mybir
from concourse.alu_op_type import AluOpType as ALU

F32 = mybir.dt.float32
F32R = mybir.dt.float32r
F16 = mybir.dt.float16
U32 = mybir.dt.uint32
ACT = mybir.ActivationFunctionType
AX = mybir.AxisListType

P = 128
D = 1024
KD = D // P
S = 512
TB = S // P
NMOD = 6
WINDOWS = (2, 4, 8, 16)
NG = len(WINDOWS)
CONV_W = 4
H = 8
DK = 256
NK = 128
K = 16
PICKS = H * K
CHUNK_C = 512
PIECES = ([("ada", j) for j in range(4)] + [("win", 1), ("ada", 4), ("ada", 5), ("win", 0), ("ada", 6), ("ada", 7)]
          + [("win", 2), ("ada", 8), ("ada", 9), ("wout", 0), ("wout", 1), ("ada", 10)]
          + [("wq", j) for j in range(4)] + [("ada", 11)])
GATE_PIECES = (4, 5, 10, 11)
SLOTS = 4
CAND_A = 4 * K
CAND = CAND_A + (K - 4) * 4
LN_EPS = 1e-5
ALPHA = 2.0 ** 0.25
LRU_C = 8.0
DROPPED = -3.0e38
PAD_P = max(WINDOWS)
PAD_C = 4
NT = NK
GT = 2
RT = 2 * GT
OUTS = 2 * TB
TOK = 8
GATE_UP = 2.0 ** 15

COLS = {}
_n = 0
for _name, _w in (("c", 8), ("ada_b", 48), ("ln0_g", 8), ("ln0_b", 8), ("ln1_g", 8), ("ln1_b", 8),
                  ("pool_scale", 4), ("conv_b", 4), ("lru_ba", 4), ("lru_bx", 4), ("lam", 4),
                  ("conv_w", 16)):
    COLS[_name] = (_n, _n + _w)
    _n += _w
NCOLS = _n
ROWS = ("ln0_g", "ln0_b", "ln1_g", "ln1_b", "ln2_g", "ln2_b", "gate1_b", "gate2_b")
C_ID, C_IOTA, C_ONE, C_MEAN, C_EPS, C_CNT = 0, P, 2 * P, 3 * P, 3 * P + 1, 3 * P + 2
NCONST = C_CNT + NG * PAD_P


class Chain:

    def __init__(self, eng, sem, reg=None, per=0):
        self.eng, self.sem, self.reg, self.per, self.n = eng, sem, reg, per, 0

    def link(self, ins):
        ins.then_inc(self.sem, 1)
        self.n += 1
        self.eng.wait_ge(self.sem, self.n if self.reg is None else self.reg * self.per + self.n)


def build(nc, x, cols, rows, consts, ada_w, w_in, w_out, wq, pool_w, wa, wx, k1t, k2t, ut, v, out):
    ctx = ExitStack()
    with ctx:
        def sb(name, shape, dt=F32):
            return ctx.enter_context(nc.sbuf_tensor(name, shape, dt))

        def sem(name):
            return ctx.enter_context(nc.semaphore(name))

        gates = nc.dram_tensor("gates_dram", [NT, P, S], F32, kind="Internal").ap()

        bank = [ctx.enter_context(nc.psum_tensor(f"bank{i}", [P, 512], F32)) for i in range(8)]
        hT = sb("hT", [P, KD, S])
        xt = sb("xt", [P, TB, D])
        row_g = sb("row_g", [P, D])
        row_b = sb("row_b", [P, D])
        row_gate = sb("row_gate", [P, D])
        cst = sb("cst", [P, NCONST])
        col = sb("col", [P, NCOLS])
        mod = sb("mod", [P, 48])
        sc = sb("sc", [P, 96])
        st = sb("st", [P, TB, 2, 6])
        mv = sb("mv", [P, TB, 2])
        sd = sb("sd", [P, TB])
        rstd = sb("rstd", [P, TB])
        ramp = sb("ramp", [P, NG, PAD_P])
        hsum = sb("hsum", [P, H, KD])
        hmean = sb("hmean", [P, H, KD])
        before = ExitStack()
        ARENA = 23552
        wbuf = before.enter_context(nc.sbuf_tensor("wbuf", [P, SLOTS * KD * CHUNK_C], F32))
        arena = before.enter_context(nc.sbuf_tensor("arena", [P, ARENA], F32))
        before.close()
        h_hi, h_lo = (sb(n, [P, KD, S], F32R) for n in ("h_hi", "h_lo"))
        u_raw = sb("u_raw", [P, RT, KD, P])
        v_raw = sb("v_raw", [P, RT, D])
        gate_in = sb("gate_in", [P, RT, S])
        u_hi, u_lo = (sb(n, [P, GT, KD, P], F32R) for n in ("u_hi", "u_lo"))
        v_hi, v_lo = (sb(n, [P, RT, D], F32R) for n in ("v_hi", "v_lo"))
        w_hi, w_lo = (sb(n, [P, RT, S], F32R) for n in ("w_hi", "w_lo"))
        gelu_out = sb("gelu_out", [P, GT, S])
        w_full = sb("w_full", [P, GT, S])
        acc = hT[:, :, :].rearrange("p (t a) n -> p t (a n)", t=TB)
        tmp = w_full[:, :, :].rearrange("p a n -> p (a n)")

        ident = cst[:, C_ID:C_ID + P]
        iota = cst[:, C_IOTA:C_IOTA + P]
        ones = cst[:, C_ONE:C_ONE + P]
        mean_col = cst[:, C_MEAN:C_MEAN + 1]
        eps = cst[:, C_EPS:C_EPS + 1]
        inv_count = cst[:, C_CNT:C_CNT + NG * PAD_P].rearrange("p (g w) -> p g w", g=NG)

        def vec(name, j=None):
            a, b = COLS[name]
            return col[:, a:b] if j is None else col[:, a + j:a + j + 1]

        silu_c = sc[:, 0:8]
        scale1, bias1, scale2, bias2 = (sc[:, 8 * n:8 * n + 8] for n in (1, 2, 3, 4))
        decay = sc[:, 40:44]
        ndecay = sc[:, 44:48]
        t4 = [sc[:, 48 + 4 * n:52 + 4 * n] for n in range(7)]

        piece_buf = wbuf[:, :].rearrange("p (s k n) -> p s k n", s=SLOTS, k=KD)

        def carve(spec):
            at, got = 0, []
            for shape in spec:
                n = 1
                for w in shape:
                    n *= w
                a = arena[:, at:at + n]
                if len(shape) == 2:
                    a = a.rearrange("p (a b) -> p a b", a=shape[0])
                if len(shape) == 3:
                    a = a.rearrange("p (a b c) -> p a b c", a=shape[0], b=shape[1])
                got.append(a)
                at += n
            assert at <= ARENA, at
            return got

        zp, zx, zg, pa, pb, xc, gr, gi, yT, pw, wab, wxb = carve(
            [(NG, PAD_P + S), (4, PAD_C + S), (4, S), (NG, PAD_P + S), (NG, PAD_P + S), (4, S), (4, S), (4, S),
             (KD, S), (NG, P), (4, P), (4, P)])
        part = arena[:, ARENA - 2 * CHUNK_C:].rearrange("p (b n) -> p b n", b=2)
        (wqc, qT, sq, keys, e1, e2, wt, vs, s_all, s_val, s_pos, s_posf, cand, c_val, c_idx, dec, eq_a, eq_b,
         pk) = carve(
            [(2, KD, DK), (2, 2, S), (2, 2, S), (2, NK), (TB, PICKS), (TB, PICKS), (TB, PICKS), (TB, PICKS),
             (2, TB, DK), (2, TB, K), (2, TB, K), (2, TB, K), (TB, CAND), (TB, K), (TB, K), (8, TB * K),
             (TB * K, K), (TB * K, K), (4, TB * H)])
        half = (P * TOK // 2,)
        stage_a, wT, *tail = carve([(P, P), (S,)] + [(S // 2,)] * 4 + [half] * 9)
        i1T, i2T, wTh, wTl, *tail = (a.bitcast(F16) for a in tail)
        key_of, *tail = (a.rearrange("p (i t) -> p i t", t=TOK) for a in tail)
        onehot1, onehot2, gate_hi, gate_lo = tail[0:2], tail[2:4], tail[4:6], tail[6:8]
        stage = [stage_a, wbuf[:, :].rearrange("p (a b) -> p a b", a=P)]

        s_x = [sem(f"x_landed{n}") for n in range(TB)]
        s_piece = [sem(f"piece_landed{n}") for n in range(SLOTS)]
        s_u = [sem(f"u_landed{n}") for n in range(RT)]
        s_v = [sem(f"v_landed{n}") for n in range(RT)]
        s_g = [sem(f"g_landed{n}") for n in range(RT)]
        s_cst, s_col, s_rows, s_gatew, s_keys, s_out = (
            sem(n) for n in ("cst_landed", "col_landed", "rows_landed", "gatew_landed", "keys_landed",
                             "out_stored"))
        s_stage = [sem(f"stage_stored{n}") for n in range(TB)]
        (s_zero, s_silu, s_modmm, s_mod, s_sc, s_aggr, s_sd, s_ln, s_tr, s_h, s_zmm, s_zev, s_poolmm, s_pooly,
         s_poolev, s_conv, s_gmm, s_sig, s_absl, s_expl, s_decay, s_a, s_th, s_bsq, s_sqrt, s_ix, s_gelu,
         s_lru, s_part, s_gatein, s_rowg, s_ymm, s_yres, s_x0mul, s_x0) = (
            sem(n) for n in (
                "pads_zeroed", "silu_made", "mod_summed", "mod_ready", "scales_ready", "stats_ready", "sd_ready",
                "normalised", "transposed", "h_ready", "z_summed", "z_ready", "pool_summed", "pool_input_ready",
                "pool_ready", "conv_ready", "gate_summed", "gate_ready", "abs_lambda_ready", "exp_lambda_ready",
                "decay_ready", "a_ready", "tanh_ready", "b_square_ready", "b_root_ready", "gated_x_ready",
                "gelu_ready", "lru_ready", "mod_part_ready", "gate_bias_landed", "gate_rows_ready", "y_summed", "y_read",
                "residual_scaled", "residual_ready"))
        (s_hmean, s_centre, s_qmm, s_qev, s_smm, s_sev, s_routed, s_eq, s_eqmul, s_e1e2, s_qsd,
         s_shift, s_exp, s_wt, s_imm, s_iev, s_hot, s_scmm, s_scev) = (
            sem(n) for n in (
                "head_mean_ready", "wq_centred", "q_summed", "q_ready", "scores_summed", "scores_ready",
                "scores_ranked", "match_ready", "match_times_index", "experts_ready",
                "q_sd_ready", "values_shifted", "exp_ready", "weights_ready", "index_transposed", "index_ready",
                "onehots_ready", "scattered", "scatter_staged"))
        s_hhi, s_hlo, s_uhi, s_ulo, s_vhi, s_vlo, s_whi, s_wlo, s_keyof = (
            sem(n) for n in ("h_hi_ready", "h_lo_ready", "u_hi_ready", "u_lo_ready", "v_hi_ready", "v_lo_ready",
                             "weighted_hi_ready", "weighted_lo_ready", "key_table_ready"))
        s_amm, s_act, s_w, s_vmm, s_acc, s_zacc, s_fsd, s_fin = (
            sem(n) for n in ("expert_summed", "expert_gelu", "expert_weighted", "value_summed", "value_added",
                             "acc_zeroed", "final_sd_ready", "output_ready"))
        s_turn = sem("ranking_turn")
        s_hot1 = sem("first_onehots_ready")
        s_cv, s_cl, s_cs, s_cf, s_ff = (sem(n) for n in ("vector_step", "route_step", "softmax_step",
                                                   "final_step", "final_stats"))

        src = {"ada": ada_w, "win": w_in, "wout": w_out, "wq": wq}
        at_piece = {p: n for n, p in enumerate(PIECES)}
        ada_order = [j for name, j in PIECES if name == "ada"]
        win_order = [j for name, j in PIECES if name == "win"]
        assert at_piece[("wq", 0)] % SLOTS == 0

        def piece(name, j):
            return piece_buf[:, at_piece[(name, j)] % SLOTS]

        def wait_piece(eng, name, j):
            n = at_piece[(name, j)]
            eng.wait_ge(s_piece[n % SLOTS], 16 * (n // SLOTS + 1))

        def used_up(n):
            name, j = PIECES[n]
            if name == "ada":
                return s_part, ada_order.index(j) + 1
            if name == "win":
                return s_zmm, 4 * (win_order.index(j) + 1)
            if name == "wout":
                return s_ymm, 2 * TB
            return s_centre, 2 * (j + 1)

        block = ctx.enter_context(nc.Block())

        @block.sync
        def _(sp):
            for tb in range(TB):
                sp.dma_start(xt[:, tb, :], x[tb * P:(tb + 1) * P, :]).then_inc(s_x[tb], 16)
            for n, (name, j) in enumerate(PIECES):
                if n >= SLOTS:
                    sp.wait_ge(*used_up(n - SLOTS))
                sp.dma_start(piece_buf[:, n % SLOTS], src[name][j]).then_inc(s_piece[n % SLOTS], 16)
            for tb in range(TB):
                sp.wait_ge(s_scev, (tb + 1) * P // 4)
                sp.dma_start(gates[:, :, tb * P:(tb + 1) * P].rearrange("i p t -> p i t"),
                             stage[tb % 2]).then_inc(s_stage[tb], 16)
            for tb in range(TB):
                sp.wait_ge(s_stage[tb], 16)

            for s in range(RT):
                sp.dma_start(u_raw[:, s], ut[s]).then_inc(s_u[s], 16)
                sp.dma_start(v_raw[:, s, :], v[s]).then_inc(s_v[s], 16)
                sp.dma_start(gate_in[:, s, :], gates[s]).then_inc(s_g[s], 16)
            with sp.Fori(0, NT // RT - 1) as i:
                for s in range(RT):
                    tile = i * RT + (RT + s)
                    sp.wait_ge(s_ulo, i * RT + (s + 1))
                    sp.dma_start(u_raw[:, s:s + 1], ut[bass.ds(tile, 1)].rearrange("a p k n -> p a k n")
                                 ).then_inc(s_u[s], 16)
                    sp.wait_ge(s_vlo, i * RT + (s + 1))
                    sp.dma_start(v_raw[:, s:s + 1, :], v[bass.ds(tile, 1)].rearrange("a p n -> p a n")
                                 ).then_inc(s_v[s], 16)
                    sp.wait_ge(s_w, i * RT + (s + 1))
                    sp.dma_start(gate_in[:, s:s + 1, :], gates[bass.ds(tile, 1)].rearrange("a p n -> p a n")
                                 ).then_inc(s_g[s], 16)
            for tb in range(TB):
                sp.wait_ge(s_fin, tb + 1)
                sp.dma_start(out[tb * P:(tb + 1) * P, :], xt[:, tb, :]).then_inc(s_out, 16)
            sp.wait_ge(s_out, 16 * TB)

        @block.gpsimd
        def _(pool):
            def load_rows(g, b):
                for row, name in ((row_g, g), (row_b, b)):
                    r = ROWS.index(name)
                    pool.dma_start(row[:, :], rows[r:r + 1, :].to_broadcast([P, D])).then_inc(s_rows, 16)

            def load_gate_bias(name):
                r = ROWS.index(name)
                pool.dma_start(row_gate[:, :], rows[r:r + 1, :].to_broadcast([P, D])).then_inc(s_gatein, 16)

            load_rows("ln0_g", "ln0_b")
            load_gate_bias("gate1_b")
            for buf in (zp[:, :, 0:PAD_P], pa[:, :, 0:PAD_P], pb[:, :, 0:PAD_P], zx[:, :, 0:PAD_C], wab, wxb):
                pool.memset(buf, 0.0).then_inc(s_zero, 1)
            pool.wait_ge(s_zero, 6)
            for dst, w in ((wab, wa), (wxb, wx)):
                for o in range(2):
                    pool.dma_start(dst[64 * o:64 * o + 64, :, 64 * o:64 * o + 64],
                                   w[o::2].rearrange("c i j -> i c j")).then_inc(s_gatew, 16)
            pool.dma_start(pw, pool_w.rearrange("g i j -> i g j")).then_inc(s_gatew, 16)

            def affine(nth):
                pool.wait_ge(s_tr, KD * (nth + 1))
                pool.wait_ge(s_rows, 32 * (nth + 1))
                for tb in range(TB):
                    pool.tensor_tensor(xt[:, tb, :], xt[:, tb, :], row_g[:, :], ALU.mult).then_inc(s_x0mul, 1)
                for tb in range(TB):
                    pool.wait_ge(s_x0mul, TB * nth + tb + 1)
                    pool.tensor_tensor(xt[:, tb, :], xt[:, tb, :], row_b[:, :], ALU.add).then_inc(s_x0, 1)
                pool.wait_ge(s_x0, TB * (nth + 1))

            affine(0)
            load_rows("ln1_g", "ln1_b")
            pool.wait_ge(s_sig, 8)
            for c in range(4):
                pool.tensor_tensor(gi[:, c, :], gi[:, c, :], xc[:, c, :], ALU.mult).then_inc(s_ix, 1)
            pool.wait_ge(s_ymm, 2 * TB)
            pool.wait_ge(s_yres, 2 * TB)
            load_gate_bias("gate2_b")

            def centre(h):
                pool.wait_ge(s_hmean, h + 1)
                if h >= 2:
                    pool.wait_ge(s_qmm, 2 * (h - 1))
                pool.tensor_tensor(
                    wqc[:, h % 2], piece("wq", h // 2)[:, :, (h % 2) * DK:(h % 2 + 1) * DK],
                    hmean[:, h, :].unsqueeze(2).to_broadcast([P, KD, DK]), ALU.add).then_inc(s_centre, 1)

            pool.dma_start(keys[:, 0, :], k1t).then_inc(s_keys, 16)
            pool.dma_start(keys[:, 1, :], k2t).then_inc(s_keys, 16)
            centre(0)
            centre(1)
            affine(1)
            load_rows("ln2_g", "ln2_b")
            for h in range(H):
                if h + 2 < H:
                    centre(h + 2)
                pool.wait_ge(s_eq, h + 1)
                eb = eq_b.rearrange("p (t j) a -> p t j a", t=TB)
                pool.tensor_tensor(eb, eb, s_posf[:, 1].unsqueeze(2).to_broadcast([P, TB, K, K]),
                                   ALU.mult).then_inc(s_eqmul, 1)
            pool.wait_ge(s_hlo, KD)
            pool.memset(acc, 0.0).then_inc(s_zacc, 1)

            def split_v(s, n):
                pool.wait_ge(s_vhi, n + 1)
                pool.tensor_tensor(v_lo[:, s, :], v_raw[:, s, :], v_hi[:, s, :].bitcast(F32), ALU.subtract
                                   ).then_inc(s_vlo, 1)

            with pool.Fori(0, NT // RT) as i:
                for s in range(RT):
                    split_v(s, i * RT + s)

        @block.scalar
        def _(act):
            act.dma_start(col[:, :], cols).then_inc(s_col, 16)
            act.dma_start(cst[:, :], consts).then_inc(s_cst, 16)
            act.wait_ge(s_col, 16)
            act.wait_ge(s_cst, 16)
            act.activation(silu_c, vec("c"), ACT.Silu).then_inc(s_silu, 1)
            act.wait_ge(s_absl, 1)
            act.activation(t4[2], t4[0], ACT.Exp, scale=-1.0).then_inc(s_expl, 1)

            def root_of_variance(nth):
                for tb in range(TB):
                    act.wait_ge(s_aggr, TB * nth + tb + 1)
                    act.activation(sd[:, tb:tb + 1], mv[:, tb, 1:2], ACT.Sqrt, bias=eps).then_inc(s_sd, 1)

            def modulate(nth, banks, scale, bias):
                act.wait_ge(s_sc, nth + 1)
                for k in range(KD):
                    act.wait_ge(s_tr, KD * nth + k + 1)
                    act.activation(hT[:, k, :], bank[banks[k % len(banks)]][:, :], ACT.Identity,
                                   bias=bias[:, k:k + 1], scale=scale[:, k:k + 1]).then_inc(s_h, 1)

            root_of_variance(0)
            modulate(0, (2, 3, 4, 5), scale1, bias1)
            act.wait_ge(s_zero, 4)
            for n in range(12):
                dst = (zx[:, n % 4, PAD_C:], zp[:, n % 4, PAD_P:], zg[:, n % 4, :])[n // 4]
                act.wait_ge(s_zmm, n + 1)
                act.activation(dst, bank[n % 2][:, :], ACT.Copy).then_inc(s_zev, 1)
            act.wait_ge(s_zev, 12)
            for c in range(4):
                act.activation(zg[:, c, :], zg[:, c, :], ACT.Gelu_apprx_tanh).then_inc(s_gelu, 1)
            for n in range(8):
                c, dst, bias = n // 2, (gr, gi)[n % 2], ("lru_ba", "lru_bx")[n % 2]
                act.wait_ge(s_gmm, n + 1)
                act.activation(dst[:, c, :], bank[4 + n % 2][:, :], ACT.Sigmoid, bias=vec(bias, c)).then_inc(s_sig, 1)
            for g in range(NG):
                act.wait_ge(s_poolmm, g + 1)
                act.activation(yT[:, g, :], bank[(6, 0)[g % 2]][:, :], ACT.Copy, scale=vec("pool_scale", g)
                               ).then_inc(s_poolev, 1)
            act.wait_ge(s_decay, 1)
            act.wait_ge(s_sig, 8)
            for c in range(4):
                act.activation(pa[:, c, PAD_P:], gr[:, c, :], ACT.Exp, scale=decay[:, c:c + 1]).then_inc(s_a, 1)
            act.wait_ge(s_a, 4)
            for c in range(4):
                act.activation(gr[:, c, :], gr[:, c, :], ACT.Tanh, scale=ndecay[:, c:c + 1]).then_inc(s_th, 1)
            for c in range(4):
                act.wait_ge(s_bsq, c + 1)
                act.activation(pb[:, c, PAD_P:], pb[:, c, PAD_P:], ACT.Sqrt).then_inc(s_sqrt, 1)
            root_of_variance(1)
            modulate(1, (4, 5), scale2, bias2)

            def queries(i, par, h, first):
                if not first:
                    act.wait_ge(s_smm, h - 1)
                for half in range(2):
                    act.wait_ge(s_qmm, h * 2 + (half + 1))
                    act.activation(qT[:, par, half, :], bank[half][:, :], ACT.Copy)
                    act.activation(sq[:, par, half, :], bank[half][:, :], ACT.Square).then_inc(s_qev, 1)

            def scores(par, h, first):
                act.wait_ge(s_smm, h + 1)
                if not first:
                    act.wait_ge(s_routed, h - 1)
                for b in range(2):
                    act.activation(s_all[:, par, 2 * b:2 * b + 2, :],
                                   bank[(2, 5)[par] + b][:, :].rearrange("p (t n) -> p t n", t=2), ACT.Copy
                                   ).then_inc(s_sev, 1)

            queries(0, 0, 0, True)
            queries(0, 1, 1, True)
            scores(0, 0, True)
            queries(1, 0, 2, False)
            scores(1, 1, True)
            with act.Fori(1, H // 2 - 1) as i:
                queries(i, 1, i * 2 + 1, False)
                scores(0, i * 2, False)
                queries(i, 0, i * 2 + 2, False)
                scores(1, i * 2 + 1, False)
            queries(3, 1, H - 1, False)
            scores(0, H - 2, False)
            scores(1, H - 1, False)
            act.activation(pk[:, 0, :], bank[4][:, 0:TB * H], ACT.Sqrt, bias=eps).then_inc(s_qsd, 1)
            act.wait_ge(s_shift, 1)
            act.activation(vs, wt, ACT.Exp).then_inc(s_exp, 1)
            for n, dst in enumerate((i1T, i2T, wT)):
                act.wait_ge(s_imm, n + 1)
                act.activation(dst, bank[n][:, :], ACT.Copy, scale=GATE_UP if n == 2 else 1.0).then_inc(s_iev, 1)
            for tb in range(TB):
                if tb >= 2:
                    act.wait_ge(s_stage[tb - 2], 16)
                with act.Fori(0, P // (2 * TOK)) as i:
                    for q in range(4):
                        act.wait_ge(s_scmm, i * 4 + (tb * P // 4 + q + 1))
                        dst = stage[tb % 2][:, :, bass.ds(i * (2 * TOK) + 4 * q, 4)].rearrange("p i t -> p t i")
                        act.activation(dst, bank[q][:, :].rearrange("p (t i) -> p t i", t=4), ACT.Copy,
                                       scale=1.0 / GATE_UP).then_inc(s_scev, 1)

            for tb in range(TB):
                act.wait_ge(s_stage[tb], 16)
            for k in range(KD):
                act.activation(h_hi[:, k, :], hT[:, k, :], ACT.Copy).then_inc(s_hhi, 1)

            def hi_u(s, n, landed, first):
                act.wait_ge(s_u[s], landed)
                if not first:
                    act.wait_ge(s_amm, n - (GT - 1))
                act.activation(u_hi[:, s % GT], u_raw[:, s], ACT.Copy).then_inc(s_uhi, 1)

            def hi_v(s, landed, free):
                act.wait_ge(s_v[s], landed)
                if free is not None:
                    act.wait_ge(s_vmm, free)
                act.activation(v_hi[:, s, :], v_raw[:, s, :], ACT.Copy).then_inc(s_vhi, 1)

            def gelu(s, n, first):
                act.wait_ge(s_amm, n + 1)
                if not first:
                    act.wait_ge(s_w, n - (GT - 1))
                act.activation(gelu_out[:, s % GT, :], bank[s][:, :], ACT.Gelu_apprx_tanh).then_inc(s_act, 1)

            def group(i, g2, first, ahead, last):
                g = i * 2 + g2
                if last:
                    return
                for j in range(GT):
                    c = (g2 + 1) * GT + j
                    hi_v(c % RT, i * 16 + 16 * (c // RT + 1), None if first else g * OUTS)
                for j in range(GT):
                    c = (g2 + 1) * GT + j
                    gelu(c % RT, i * RT + c, False)
                    if ahead:
                        c += GT
                        hi_u(c % RT, i * RT + c, i * 16 + 16 * (c // RT + 1), False)

            for j in range(GT):
                hi_u(j, j, 16, True)
            for j in range(GT):
                hi_v(j, 16, None)
            for j in range(GT):
                gelu(j, j, True)
                hi_u(GT + j, GT + j, 16, False)
            group(0, 0, True, True, False)
            group(0, 1, False, True, False)
            with act.Fori(1, NT // RT - 1) as i:
                group(i, 0, False, True, False)
                group(i, 1, False, True, False)
            group(NT // RT - 1, 0, False, False, False)
            for tb in range(TB):
                act.wait_ge(s_ff, tb + 1)
                act.activation(sd[:, tb:tb + 1], mv[:, tb, 1:2], ACT.Sqrt, bias=eps).then_inc(s_fsd, 1)

        @block.tensor
        def _(pe):
            def modulation(j):
                n = ada_order.index(j)
                pe.wait_ge(s_part, n + 1)
                if j in GATE_PIECES:
                    mm = pe.matmul(bank[(6, 3)[j % 2]][:, :], ones, part[:, n % 2, :], start=True, stop=True)
                else:
                    for m in range(4):
                        mm = pe.matmul(bank[7][:, 4 * j + m:4 * j + m + 1], part[:, n % 2, m * P:(m + 1) * P],
                                       ones[:, 0:1], start=True, stop=True)
                mm.then_inc(s_modmm, 1)

            def transposes(nth, banks, chunks=range(KD)):
                pe.wait_ge(s_ln, TB * (nth + 1))
                for k in chunks:
                    if k >= len(banks):
                        pe.wait_ge(s_h, KD * nth + k - len(banks) + 1)
                    for tb in range(TB):
                        mm = pe.transpose(bank[banks[k % len(banks)]][:, tb * P:(tb + 1) * P],
                                          xt[:, tb, k * P:(k + 1) * P], ident)
                    mm.then_inc(s_tr, 1)

            pe.wait_ge(s_cst, 16)
            transposes(0, (2, 3, 4, 5), range(4))
            for j in range(4):
                modulation(j)
            transposes(0, (2, 3, 4, 5), range(4, KD))
            pe.wait_ge(s_h, KD)
            for n in range(12):
                wait_piece(pe, "win", win_order[n // 4])
                if n >= 2:
                    pe.wait_ge(s_zev, n - 1)
                for k in range(KD):
                    mm = pe.matmul(bank[n % 2][:, :], piece("win", win_order[n // 4])[:, k, (n % 4) * P:(n % 4 + 1) * P],
                                   hT[:, k, :], start=(k == 0), stop=(k == KD - 1))
                mm.then_inc(s_zmm, 1)
                if n % 4 == 3:
                    modulation(4 + n // 2 - 1)
                    modulation(4 + n // 2)
            pe.wait_ge(s_gatew, 80)
            for n in range(8):
                c = n // 2
                pe.wait_ge(s_conv, c + 1)
                if n >= 2:
                    pe.wait_ge(s_sig, n - 1)
                pe.matmul(bank[4 + n % 2][:, :], (wab, wxb)[n % 2][:, c, :], xc[:, c, :], start=True, stop=True
                          ).then_inc(s_gmm, 1)
            pe.wait_ge(s_zev, 12)
            pe.wait_ge(s_rowg, 2)
            for g in range(NG):
                pe.wait_ge(s_pooly, g + 1)
                if g >= 2:
                    pe.wait_ge(s_poolev, g - 1)
                pe.matmul(bank[(6, 0)[g % 2]][:, :], pw[:, g, :], (pa, pb)[g % 2][:, g, PAD_P:],
                          start=True, stop=True).then_inc(s_poolmm, 1)
            pe.wait_ge(s_poolev, NG)
            pe.wait_ge(s_lru, 4)
            wait_piece(pe, "wout", 0)
            wait_piece(pe, "wout", 1)
            for n in range(2 * TB):
                if n >= 4:
                    pe.wait_ge(s_yres, n - 3)
                for k in range(KD):
                    mm = pe.matmul(bank[n % 4][:, :], yT[:, k, (n // 2) * P:(n // 2 + 1) * P],
                                   piece("wout", n % 2)[:, k, :], start=(k == 0), stop=(k == KD - 1))
                mm.then_inc(s_ymm, 1)
            transposes(1, (4, 5))

            def queries(par, h, first):
                pe.wait_ge(s_centre, h + 1)
                for half in range(2):
                    if not first:
                        pe.wait_ge(s_qev, h * 2 + (half - 1))
                    for k in range(KD):
                        mm = pe.matmul(bank[half][:, :], wqc[:, par, k, half * P:(half + 1) * P], hT[:, k, :],
                                       start=(k == 0), stop=(k == KD - 1))
                    mm.then_inc(s_qmm, 1)

            def scores(par, h, first, var_at):
                pe.wait_ge(s_qev, h * 2 + 2)
                if not first:
                    pe.wait_ge(s_sev, h * 2 - 2)
                for tb in range(TB):
                    for half in range(2):
                        at = (tb % 2) * DK + half * NK
                        pe.matmul(bank[(2, 5)[par] + tb // 2][:, at:at + NK],
                                  qT[:, par, half, tb * P:(tb + 1) * P], keys[:, half, :], start=True, stop=True)
                for tb in range(TB):
                    for half in range(2):
                        mm = pe.matmul(bank[4][:, var_at(tb)], sq[:, par, half, tb * P:(tb + 1) * P], mean_col,
                                       start=(half == 0), stop=(half == 1))
                mm.then_inc(s_smm, 1)

            def static_at(h):
                return lambda tb: slice(h * TB + tb, h * TB + tb + 1)

            def register_at(h):
                return lambda tb: bass.ds(h * TB + tb, 1)

            pe.wait_ge(s_h, 2 * KD)
            pe.wait_ge(s_yres, 2 * TB)
            queries(0, 0, True)
            queries(1, 1, False)
            pe.wait_ge(s_keys, 32)
            scores(0, 0, True, static_at(0))
            queries(0, 2, False)
            scores(1, 1, True, static_at(1))
            for i in range(1, H // 2 - 1):
                queries(1, i * 2 + 1, False)
                scores(0, i * 2, False, static_at(i * 2))
                queries(0, i * 2 + 2, False)
                scores(1, i * 2 + 1, False, static_at(i * 2 + 1))
            queries(1, H - 1, False)
            scores(0, H - 2, False, static_at(H - 2))
            scores(1, H - 1, False, static_at(H - 1))
            pe.wait_ge(s_qev, 2 * H)
            pe.wait_ge(s_sev, 2 * H)
            pe.wait_ge(s_wt, 1)
            pe.wait_ge(s_e1e2, H)
            for n, m in enumerate((e1, e2, wt)):
                for tb in range(TB):
                    mm = pe.transpose(bank[n][:, tb * P:(tb + 1) * P], m[:, tb, :], ident)
                mm.then_inc(s_imm, 1)
            pe.wait_ge(s_iev, 3)
            modulation(10)
            modulation(11)
            pe.wait_ge(s_rowg, 4)

            def scatter(i, first):
                for q in range(4):
                    pe.wait_ge(s_hot, i * 2 + (q // 2 + 1))
                    if not first:
                        pe.wait_ge(s_scev, i * 4 + (q - 3))
                    for t in range(4):
                        at, b = 4 * (q % 2) + t, q // 2
                        pe.matmul(bank[q][:, t * P:(t + 1) * P], onehot2[b][:, :, at], gate_hi[b][:, :, at],
                                  start=True, stop=False)
                        mm = pe.matmul(bank[q][:, t * P:(t + 1) * P], onehot2[b][:, :, at], gate_lo[b][:, :, at],
                                       start=False, stop=True)
                    mm.then_inc(s_scmm, 1)

            scatter(0, True)
            with pe.Fori(1, S // (2 * TOK)) as i:
                scatter(i, False)

            def thrice(out, k, n, pairs):
                (a_hi, a_lo), (b_hi, b_lo) = pairs
                pe.matmul(out, a_hi, b_hi, start=(k == 0), stop=False)
                pe.matmul(out, a_hi, b_lo, start=False, stop=False)
                return pe.matmul(out, a_lo, b_hi, start=False, stop=(k == n - 1))

            def expert_inputs(s, n, first):
                pe.wait_ge(s_ulo, n + 1)
                if not first:
                    pe.wait_ge(s_act, n - (RT - 1))
                for k in range(KD):
                    mm = thrice(bank[s][:, :], k, KD, ((u_hi[:, s % GT, k, :], u_lo[:, s % GT, k, :]),
                                                       (h_hi[:, k, :], h_lo[:, k, :])))
                mm.then_inc(s_amm, 1)

            def values(g2, o, n, first):
                t, d = slice(o // 2 * P, (o // 2 + 1) * P), slice(o % 2 * 512, (o % 2 + 1) * 512)
                if not first:
                    pe.wait_ge(s_acc, n - 3)
                for j in range(GT):
                    s = GT * g2 + j
                    mm = thrice(bank[4 + o % 4][:, :], j, GT, ((w_hi[:, s, t], w_lo[:, s, t]),
                                                               (v_hi[:, s, d], v_lo[:, s, d])))
                mm.then_inc(s_vmm, 1)

            def group(i, g2, first, last):
                g = i * 2 + g2
                for j in range(GT):
                    if not last:
                        c = (g2 + 1) * GT + j
                        expert_inputs(c % RT, i * RT + c, first and c < RT)
                    if j == 0:
                        pe.wait_ge(s_wlo, g * GT + GT)
                        pe.wait_ge(s_vlo, g * GT + GT)
                    for o in range(j * OUTS // GT, (j + 1) * OUTS // GT):
                        values(g2, o, g * OUTS + o, first and o < 4)

            pe.wait_ge(s_scev, S // 4)
            pe.wait_ge(s_hlo, KD)
            for j in range(GT):
                expert_inputs(j, j, True)
            group(0, 0, True, False)
            group(0, 1, False, False)
            with pe.Fori(1, NT // RT - 1) as i:
                group(i, 0, False, False)
                group(i, 1, False, False)
            group(NT // RT - 1, 0, False, False)
            group(NT // RT - 1, 1, False, True)

        @block.vector
        def _(ve):
            steps = Chain(ve, s_cv)
            link = steps.link

            def block_stats(tb):
                for b in range(2):
                    last = ve.bn_stats(st[:, tb, b, :], xt[:, tb, b * 512:(b + 1) * 512])
                link(last)
                ve.bn_aggr(mv[:, tb, :], st[:, tb, :, :]).then_inc(s_aggr, 1)

            def normalise(nth, tb):
                ve.wait_ge(s_sd, TB * nth + tb + 1)
                link(ve.reciprocal(rstd[:, tb:tb + 1], sd[:, tb:tb + 1]))
                ve.wait_ge(s_aggr, TB * nth + tb + 1)
                ve.tensor_scalar(xt[:, tb, :], xt[:, tb, :], mv[:, tb, 0:1], rstd[:, tb:tb + 1],
                                 ALU.subtract, ALU.mult).then_inc(s_ln, 1)

            def partial_modulation(j):
                n = ada_order.index(j)
                wait_piece(ve, "ada", j)
                if n >= 2:
                    ve.wait_ge(s_modmm, n - 1)
                for k in range(KD):
                    if k == 0:
                        link(ve.tensor_scalar(part[:, n % 2, :], piece("ada", j)[:, k, :], silu_c[:, k:k + 1],
                                              None, ALU.mult))
                        continue
                    last = ve.scalar_tensor_tensor(out=part[:, n % 2, :], in0=piece("ada", j)[:, k, :],
                                                   scalar=silu_c[:, k:k + 1], in1=part[:, n % 2, :],
                                                   op0=ALU.mult, op1=ALU.add)
                    if k < KD - 1:
                        link(last)
                last.then_inc(s_part, 1)

            def add_gate_row(nth):
                ve.wait_ge(s_gatein, 16 * (nth + 1))
                for b in range(2):
                    ve.wait_ge(s_modmm, ada_order.index(GATE_PIECES[2 * nth + b]) + 1)
                    part_row = row_gate[:, b * 512:(b + 1) * 512]
                    ve.tensor_tensor(part_row, part_row, bank[(6, 3)[b]][:, :], ALU.add).then_inc(s_rowg, 1)

            def read_mod(a, b, pieces):
                ve.wait_ge(s_modmm, pieces)
                o = COLS["ada_b"][0]
                link(ve.tensor_tensor(mod[:, a:b], bank[7][:, a:b], col[:, o + a:o + b], ALU.add))

            def scales(shift, scale, g, b, out_scale, out_bias):
                ve.scalar_tensor_tensor(out=out_scale, in0=mod[:, scale:scale + 8], scalar=1.0, in1=vec(g),
                                        op0=ALU.add, op1=ALU.mult)
                link(ve.scalar_tensor_tensor(out=out_bias, in0=mod[:, scale:scale + 8], scalar=1.0, in1=vec(b),
                                             op0=ALU.add, op1=ALU.mult))
                ve.tensor_tensor(out_bias, out_bias, mod[:, shift:shift + 8], ALU.add).then_inc(s_sc, 1)

            ve.wait_ge(s_col, 16)
            lam, (al, m, e, r, z, z2, p) = vec("lam"), t4
            ve.tensor_scalar(m, lam, -1.0, 0.0, ALU.mult, ALU.max)
            ve.scalar_tensor_tensor(out=al, in0=lam, scalar=-1.0, in1=lam, op0=ALU.mult, op1=ALU.max
                                    ).then_inc(s_absl, 1)
            for tb in range(TB):
                ve.wait_ge(s_x[tb], 16)
                block_stats(tb)
            for tb in range(TB):
                normalise(0, tb)
            ve.wait_ge(s_silu, 1)
            for j in range(4):
                partial_modulation(j)
            read_mod(0, 16, 4)
            scales(0, 8, "ln0_g", "ln0_b", scale1, bias1)
            partial_modulation(4)
            partial_modulation(5)
            ve.wait_ge(s_expl, 1)
            link(ve.tensor_scalar(z, e, 2.0, None, ALU.add))
            link(ve.reciprocal(r, z))
            link(ve.tensor_tensor(z, e, r, ALU.mult))
            link(ve.tensor_tensor(z2, z, z, ALU.mult))
            link(ve.tensor_scalar(p, z2, 1.0 / 19, None, ALU.mult))
            for n in range(17, 1, -2):
                link(ve.scalar_tensor_tensor(out=p, in0=p, scalar=1.0 / n, in1=z2, op0=ALU.add, op1=ALU.mult))
            link(ve.scalar_tensor_tensor(out=p, in0=p, scalar=1.0, in1=z, op0=ALU.add, op1=ALU.mult))
            link(ve.scalar_tensor_tensor(out=p, in0=p, scalar=2.0, in1=m, op0=ALU.mult, op1=ALU.add))
            ve.tensor_scalar(decay, p, -LRU_C, None, ALU.mult)
            ve.tensor_scalar(ndecay, p, LRU_C, None, ALU.mult).then_inc(s_decay, 1)

            ve.wait_ge(s_zero, 6)
            for t in range(CONV_W):
                for c in range(4):
                    w = vec("conv_w", 4 * t + c)
                    shifted = zx[:, c, PAD_C - CONV_W + 1 + t:PAD_C - CONV_W + 1 + t + S]
                    if t == 0:
                        ve.wait_ge(s_zev, c + 1)
                        last = ve.tensor_scalar(xc[:, c, :], shifted, w, vec("conv_b", c), ALU.mult, ALU.add)
                    else:
                        last = ve.scalar_tensor_tensor(out=xc[:, c, :], in0=shifted, scalar=w, in1=xc[:, c, :],
                                                       op0=ALU.mult, op1=ALU.add)
                    if t == CONV_W - 1:
                        last.then_inc(s_conv, 1)
                if t < CONV_W - 1:
                    link(last)
            add_gate_row(0)
            partial_modulation(6)
            partial_modulation(7)
            ve.wait_ge(s_zev, 8)
            bufs = (zp, pa, pb, pa, pb)
            for n, w in enumerate(WINDOWS):
                a, b = bufs[n], bufs[n + 1]
                link(ve.tensor_tensor(b[:, n:, PAD_P:], a[:, n:, PAD_P:], a[:, n:, PAD_P - w // 2:PAD_P - w // 2 + S],
                                      ALU.add))
            for g, w in enumerate(WINDOWS):
                last = ve.tensor_tensor(ramp[:, g, :], bufs[g + 1][:, g, PAD_P:2 * PAD_P], inv_count[:, g, :], ALU.mult)
            link(last)
            for g, w in enumerate(WINDOWS):
                b = bufs[g + 1][:, g, PAD_P:]
                last = ve.scalar_tensor_tensor(out=b, in0=b, scalar=1.0 / w, in1=zp[:, g, PAD_P:],
                                               op0=ALU.mult, op1=ALU.subtract)
            link(last)
            for g in range(NG):
                ve.tensor_tensor(bufs[g + 1][:, g, PAD_P:2 * PAD_P], ramp[:, g, :], zp[:, g, PAD_P:2 * PAD_P],
                                 ALU.subtract).then_inc(s_pooly, 1)
            partial_modulation(8)
            partial_modulation(9)
            ve.wait_ge(s_poolmm, NG)
            for c in range(4):
                ve.wait_ge(s_a, c + 1)
                last = ve.tensor_tensor(pb[:, c, PAD_P:], pa[:, c, PAD_P:], pa[:, c, PAD_P:], ALU.mult)
            link(last)
            for c in range(4):
                ve.wait_ge(s_th, c + 1)
                ve.scalar_tensor_tensor(out=pb[:, c, PAD_P:], in0=pb[:, c, PAD_P:], scalar=1.0, in1=gr[:, c, :],
                                        op0=ALU.add, op1=ALU.mult).then_inc(s_bsq, 1)
            for c in range(4):
                ve.wait_ge(s_sqrt, c + 1)
                ve.wait_ge(s_ix, c + 1)
                last = ve.tensor_tensor(pb[:, c, PAD_P:], pb[:, c, PAD_P:], gi[:, c, :], ALU.mult)
            link(last)
            ve.wait_ge(s_ix, 4)
            for c in range(4):
                last = ve.tensor_tensor_scan(xc[:, c, :], pa[:, c, PAD_P:], pb[:, c, PAD_P:], 0.0, ALU.mult, ALU.add)
            link(last)
            ve.wait_ge(s_gelu, 4)
            for c in range(4):
                ve.tensor_tensor(yT[:, NG + c, :], xc[:, c, :], zg[:, c, :], ALU.mult).then_inc(s_lru, 1)
            read_mod(24, 40, 10)
            scales(24, 32, "ln1_g", "ln1_b", scale2, bias2)
            ve.wait_ge(s_rowg, 2)
            ve.wait_ge(s_x0, TB)
            ve.wait_ge(s_lru, 4)
            partial_modulation(10)
            for tb in range(TB):
                for half in range(2):
                    n = 2 * tb + half
                    ve.wait_ge(s_ymm, n + 1)
                    ve.tensor_tensor(zg[:, n % 4, :], bank[n % 4][:, :], row_gate[:, half * 512:(half + 1) * 512],
                                     ALU.mult).then_inc(s_yres, 1)
                ve.wait_ge(s_yres, 2 * tb + 2)
                for half in range(2):
                    piece_x = xt[:, tb, half * 512:(half + 1) * 512]
                    last = ve.scalar_tensor_tensor(out=piece_x, in0=piece_x, scalar=ALPHA,
                                                   in1=zg[:, (2 * tb + half) % 4, :], op0=ALU.mult, op1=ALU.add)
                link(last)
                block_stats(tb)
                if tb:
                    normalise(1, tb - 1)
            normalise(1, TB - 1)

            def head_means(i):
                for par in range(2):
                    w = piece_buf[:, bass.ds(i, 1), :, par * DK:(par + 1) * DK]
                    last = ve.tensor_reduce(hsum[:, bass.ds(i * 2 + par, 1), :], w, AX.X, ALU.add)
                return last

            def scaled_means(i):
                last = ve.tensor_scalar(hmean[:, bass.ds(i * 2, 1), :], hsum[:, bass.ds(i * 2, 1), :],
                                        -1.0 / DK, None, ALU.mult).then_inc(s_hmean, 1)
                ve.tensor_scalar(hmean[:, bass.ds(i * 2 + 1, 1), :], hsum[:, bass.ds(i * 2 + 1, 1), :],
                                 -1.0 / DK, None, ALU.mult).then_inc(s_hmean, 1)

            def top_k(parts, step, done=None):
                for val, idx, data in parts:
                    last = ve.max(val[:, 0:8], data)
                step(last)
                for val, idx, data in parts:
                    ve.max_index(idx[:, 0:8], val[:, 0:8], data)
                for val, idx, data in parts:
                    last = ve.match_replace(data, val[:, 0:8], data, DROPPED)
                step(last)
                for val, idx, data in parts:
                    last = ve.max(val[:, 8:16], data)
                step(last)
                for val, idx, data in parts:
                    last = ve.max_index(idx[:, 8:16], val[:, 8:16], data)
                return last

            ci = c_idx.rearrange("p t k -> p (t k)").bitcast(U32)
            dci = [dec[:, n, :].bitcast(U32) for n in range(4)]
            ka, kb, low = dec[:, 4, :], dec[:, 5, :], dec[:, 6, :]
            iota16 = iota[:, 0:K].unsqueeze(1).to_broadcast([P, TB * K, K])

            def route(par, h, chain):
                def step(ins):
                    chain.link(ins)
                    ve.sem_inc(s_turn, 1)

                ve.wait_ge(s_sev, h * 2 + 2)
                ve.sem_inc(s_turn, 1)
                last = top_k([(s_val[:, half, tb, :], s_pos[:, half, tb, :].bitcast(U32),
                               s_all[:, par, tb, half * NK:(half + 1) * NK])
                              for tb in range(TB) for half in range(2)], step)
                last.then_inc(s_routed, 1)
                ve.wait_ge(s_routed, h + 1)
                ve.tensor_copy(s_posf, s_pos.bitcast(U32))
                ve.tensor_tensor(cand[:, :, 0:CAND_A].rearrange("p t (a b) -> p t a b", a=4),
                                 s_val[:, 0, :, 0:4].unsqueeze(3).to_broadcast([P, TB, 4, K]),
                                 s_val[:, 1, :, :].unsqueeze(2).to_broadcast([P, TB, 4, K]), ALU.add)
                step(ve.tensor_tensor(cand[:, :, CAND_A:].rearrange("p t (a b) -> p t a b", a=K - 4),
                                      s_val[:, 0, :, 4:].unsqueeze(3).to_broadcast([P, TB, K - 4, 4]),
                                      s_val[:, 1, :, 0:4].unsqueeze(2).to_broadcast([P, TB, K - 4, 4]), ALU.add))
                step(top_k([(c_val[:, tb, :], c_idx[:, tb, :].bitcast(U32), cand[:, tb, :]) for tb in range(TB)], step))
                ve.tensor_copy(vs[:, :, bass.ds(h * K, K)], c_val)
                ve.tensor_scalar(dci[0], ci, 2, None, ALU.logical_shift_right)
                ve.tensor_scalar(dci[1], ci, 4, None, ALU.logical_shift_right)
                ve.tensor_scalar(dci[2], ci, 12, None, ALU.bitwise_and)
                step(ve.tensor_scalar(dci[3], ci, 3, None, ALU.bitwise_and))
                ve.scalar_tensor_tensor(out=ka, in0=dci[0], scalar=-12.0, in1=dci[1], op0=ALU.add, op1=ALU.max)
                step(ve.scalar_tensor_tensor(out=low, in0=ci, scalar=float(CAND_A), in1=dci[2],
                                             op0=ALU.is_lt, op1=ALU.mult))
                step(ve.tensor_tensor(kb, low, dci[3], ALU.add))
                ve.tensor_tensor(eq_b, kb.unsqueeze(2).to_broadcast([P, TB * K, K]), iota16, ALU.is_equal
                                 ).then_inc(s_eq, 1)
                step(ve.tensor_tensor(eq_a, ka.unsqueeze(2).to_broadcast([P, TB * K, K]), iota16, ALU.is_equal))
                ea = eq_a.rearrange("p (t j) a -> p t j a", t=TB)
                eb = eq_b.rearrange("p (t j) a -> p t j a", t=TB)
                step(ve.tensor_tensor(ea, ea, s_posf[:, 0].unsqueeze(2).to_broadcast([P, TB, K, K]), ALU.mult))
                ve.tensor_reduce(e1[:, :, bass.ds(h * K, K)], ea, AX.X, ALU.add)
                ve.wait_ge(s_eqmul, h + 1)
                ve.tensor_reduce(e2[:, :, bass.ds(h * K, K)], eb, AX.X, ALU.add).then_inc(s_e1e2, 1)

            for j in range(4):
                wait_piece(ve, "wq", j)
            link(head_means(0))
            scaled_means(0)
            per = 1 + 2 * STEPS_ROUTE
            with ve.Fori(0, H // 2 - 1) as i:
                chain = Chain(ve, s_cl, i, per)
                chain.link(head_means(i + 1))
                scaled_means(i + 1)
                route(0, i * 2, chain)
                route(1, i * 2 + 1, chain)
                assert chain.n == per, chain.n
            chain = Chain(ve, s_cl)
            chain.n = (H // 2 - 1) * per
            route(0, H - 2, chain)
            route(1, H - 1, chain)

            link = Chain(ve, s_cs).link
            ve.wait_ge(s_qsd, 1)
            link(ve.reciprocal(pk[:, 1, :], pk[:, 0, :]))
            v4 = vs.rearrange("p t (h k) -> p t h k", h=H)
            w4 = wt.rearrange("p t (h k) -> p t h k", h=H)
            full = [P, TB, H, K]
            link(ve.tensor_tensor(v4, v4, pk[:, 1, :].rearrange("p (h t) -> p t h", h=H).unsqueeze(3).to_broadcast(full),
                                  ALU.mult))
            ve.tensor_tensor(w4, v4, v4[:, :, :, 0:1].to_broadcast(full), ALU.subtract).then_inc(s_shift, 1)
            ve.wait_ge(s_exp, 1)
            link(ve.tensor_reduce(pk[:, 2, :].rearrange("p (t h) -> p t h", t=TB), v4, AX.X, ALU.add))
            link(ve.reciprocal(pk[:, 3, :], pk[:, 2, :]))
            ve.tensor_tensor(w4, v4, pk[:, 3, :].rearrange("p (t h) -> p t h", t=TB).unsqueeze(3).to_broadcast(full),
                             ALU.mult).then_inc(s_wt, 1)
            link = steps.link
            partial_modulation(11)
            add_gate_row(1)

            ve.wait_ge(s_iev, 3)
            ve.tensor_copy(key_of, iota.unsqueeze(2).to_broadcast([P, P, TOK]))
            ve.tensor_copy(wTh, wT).then_inc(s_keyof, 1)
            ve.wait_ge(s_keyof, 1)
            ve.tensor_tensor(wTl, wT, wTh, ALU.subtract).then_inc(s_keyof, 1)
            ve.wait_ge(s_keyof, 2)

            def onehots(i, b, first):
                def of(table):
                    return table[:, bass.ds(i * (2 * TOK) + b * TOK, TOK)].unsqueeze(1).to_broadcast([P, P, TOK])

                if not first:
                    ve.wait_ge(s_scmm, i * 4 + (2 * b - 2))
                ve.tensor_tensor(onehot1[b], key_of, of(i1T), ALU.is_equal).then_inc(s_hot1, 1)
                ve.tensor_tensor(onehot2[b], key_of, of(i2T), ALU.is_equal)
                ve.wait_ge(s_hot1, i * 2 + (b + 1))
                ve.tensor_tensor(gate_hi[b], onehot1[b], of(wTh), ALU.mult)
                ve.tensor_tensor(gate_lo[b], onehot1[b], of(wTl), ALU.mult).then_inc(s_hot, 1)

            for b in range(2):
                onehots(0, b, True)
            with ve.Fori(1, S // (2 * TOK)) as i:
                for b in range(2):
                    onehots(i, b, False)

            for k in range(KD):
                ve.wait_ge(s_hhi, k + 1)
                ve.tensor_tensor(h_lo[:, k, :], hT[:, k, :], h_hi[:, k, :].bitcast(F32), ALU.subtract
                                 ).then_inc(s_hlo, 1)

            def split_u(s, n):
                ve.wait_ge(s_uhi, n + 1)
                ve.tensor_tensor(u_lo[:, s % GT], u_raw[:, s], u_hi[:, s % GT].bitcast(F32), ALU.subtract
                                 ).then_inc(s_ulo, 1)

            def weigh(s, n, landed, free):
                j = s % GT
                ve.wait_ge(s_act, n + 1)
                ve.wait_ge(s_g[s], landed)
                ve.tensor_tensor(w_full[:, j, :], gelu_out[:, j, :], gate_in[:, s, :], ALU.mult).then_inc(s_w, 1)
                if free is not None:
                    ve.wait_ge(s_vmm, free)
                ve.wait_ge(s_w, n + 1)
                ve.tensor_copy(w_hi[:, s, :], w_full[:, j, :]).then_inc(s_whi, 1)
                ve.wait_ge(s_whi, n + 1)
                ve.tensor_tensor(w_lo[:, s, :], w_full[:, j, :], w_hi[:, s, :].bitcast(F32), ALU.subtract
                                 ).then_inc(s_wlo, 1)

            def add_up(o, n):
                ve.wait_ge(s_vmm, n + 1)
                part = acc[:, o // 2, (o % 2) * 512:(o % 2 + 1) * 512]
                ve.tensor_tensor(part, part, bank[4 + o % 4][:, :], ALU.add).then_inc(s_acc, 1)

            def group(i, g2, first, ahead, last):
                g = i * 2 + g2
                if not first:
                    ve.wait_ge(s_acc, g * OUTS)
                for j in range(GT):
                    if not last:
                        c = (g2 + 1) * GT + j
                        weigh(c % RT, i * RT + c, i * 16 + 16 * (c // RT + 1), None if first else g * OUTS)
                        if ahead:
                            c += GT
                            split_u(c % RT, i * RT + c)
                    for o in range(j * OUTS // GT, (j + 1) * OUTS // GT):
                        add_up(o, g * OUTS + o)

            for j in range(GT):
                split_u(j, j)
            for j in range(GT):
                weigh(j, j, 16, None)
                split_u(GT + j, GT + j)
            ve.wait_ge(s_zacc, 1)
            group(0, 0, True, True, False)
            group(0, 1, False, True, False)
            with ve.Fori(1, NT // RT - 1) as i:
                group(i, 0, False, True, False)
                group(i, 1, False, True, False)
            group(NT // RT - 1, 0, False, False, False)
            group(NT // RT - 1, 1, False, False, True)

            ve.wait_ge(s_acc, NT // GT * OUTS)
            ve.wait_ge(s_rowg, 4)
            ve.wait_ge(s_x0, 2 * TB)
            ve.wait_ge(s_rows, 96)
            link = Chain(ve, s_cf).link
            for tb in range(TB):
                link(ve.tensor_tensor(tmp, acc[:, tb, :], row_gate[:, :], ALU.mult))
                link(ve.scalar_tensor_tensor(out=xt[:, tb, :], in0=xt[:, tb, :], scalar=ALPHA, in1=tmp,
                                             op0=ALU.mult, op1=ALU.add))
                for b in range(2):
                    last = ve.bn_stats(st[:, tb, b, :], xt[:, tb, b * 512:(b + 1) * 512])
                link(last)
                ve.bn_aggr(mv[:, tb, :], st[:, tb, :, :]).then_inc(s_ff, 1)
            for tb in range(TB):
                ve.wait_ge(s_fsd, tb + 1)
                link(ve.reciprocal(rstd[:, tb:tb + 1], sd[:, tb:tb + 1]))
                link(ve.tensor_scalar(xt[:, tb, :], xt[:, tb, :], mv[:, tb, 0:1], rstd[:, tb:tb + 1],
                                      ALU.subtract, ALU.mult))
                link(ve.tensor_tensor(xt[:, tb, :], xt[:, tb, :], row_g[:, :], ALU.mult))
                ve.tensor_tensor(xt[:, tb, :], xt[:, tb, :], row_b[:, :], ALU.add).then_inc(s_fin, 1)


STEPS_ROUTE = 13


def constants():
    import numpy as np

    a = np.zeros((P, NCONST), np.float32)
    a[:, C_ID:C_ID + P] = np.eye(P)
    a[:, C_IOTA:C_IOTA + P] = np.arange(P)
    a[:, C_ONE:C_ONE + P] = 1.0
    a[:, C_MEAN] = 1.0 / DK
    a[:, C_EPS] = LN_EPS
    for g, w in enumerate(WINDOWS):
        for t in range(PAD_P):
            a[:, C_CNT + g * PAD_P + t] = 1.0 / min(t + 1, w)
    return a


def kernel(x, c, ln0_g, ln0_b, ada_w, ada_b, w_in, pool_w, pool_scale, conv_w, conv_b,
           lru_wa, lru_ba, lru_wx, lru_bx, lru_lambda, w_out, ln1_g, ln1_b,
           peer_wq, peer_k1, peer_k2, peer_u, peer_v, ln2_g, ln2_b):
    import numpy as np
    import concourse.bacc as bacc
    from concourse.bass_utils import run_bass_kernel_spmd

    def chunks(a):
        return np.asarray(a).reshape(-1, P).T

    def pieces(w):
        w = np.asarray(w).reshape(KD, P, -1, CHUNK_C)
        return np.ascontiguousarray(w.transpose(2, 1, 0, 3))

    cols = np.concatenate([chunks(a) for a in (
        c, ada_b, ln0_g, ln0_b, ln1_g, ln1_b, pool_scale, conv_b, lru_ba, lru_bx, lru_lambda, conv_w)], axis=1)
    rows = np.stack([np.asarray(a).reshape(D) for a in (
        ln0_g, ln0_b, ln1_g, ln1_b, ln2_g, ln2_b, np.asarray(ada_b)[0, 2 * D:3 * D], np.asarray(ada_b)[0, 5 * D:])])
    arrays = {
        "x": np.asarray(x)[0], "cols": cols, "rows": rows, "consts": constants(),
        "ada_w": pieces(ada_w), "w_in": pieces(w_in), "w_out": pieces(w_out), "wq": pieces(peer_wq),
        "pool_w": np.asarray(pool_w)[0], "wa": np.asarray(lru_wa)[0], "wx": np.asarray(lru_wx)[0],
        "k1t": np.asarray(peer_k1)[0].T, "k2t": np.asarray(peer_k2)[0].T,
        "ut": np.asarray(peer_u)[0].reshape(NT, P, KD, P).transpose(0, 3, 2, 1),
        "v": np.asarray(peer_v)[0].reshape(NT, P, D),
    }
    arrays = {n: np.ascontiguousarray(a) for n, a in arrays.items()}
    nc = bacc.Bacc("TRN2", target_bir_lowering=False, num_devices=1)
    ins = {n: nc.dram_tensor(n + "_dram", a.shape, F32, kind="ExternalInput").ap() for n, a in arrays.items()}
    out = nc.dram_tensor("out_dram", (S, D), F32, kind="ExternalOutput").ap()
    build(nc, *(ins[n] for n in ("x", "cols", "rows", "consts", "ada_w", "w_in", "w_out", "wq", "pool_w",
                                 "wa", "wx", "k1t", "k2t", "ut", "v")), out)
    r = run_bass_kernel_spmd(nc, [{n + "_dram": a for n, a in arrays.items()}], core_ids=[0])
    return r.results[0]["out_dram"].reshape(1, S, D)
```

```python
from contextlib import ExitStack

import concourse.bass as bass
from concourse import mybir
from concourse.alu_op_type import AluOpType as ALU

F32 = mybir.dt.float32
F32R = mybir.dt.float32r
F16 = mybir.dt.float16
U32 = mybir.dt.uint32
ACT = mybir.ActivationFunctionType
AX = mybir.AxisListType

P = 128
D = 1024
KD = D // P
S = 512
TB = S // P
NMOD = 6
WINDOWS = (2, 4, 8, 16)
NG = len(WINDOWS)
CONV_W = 4
H = 8
DK = 256
NK = 128
K = 16
PICKS = H * K
CHUNK_C = 512
PIECES = ([("ada", j) for j in range(4)] + [("win", 1), ("ada", 4), ("ada", 5), ("win", 0), ("ada", 6), ("ada", 7)]
          + [("win", 2), ("ada", 8), ("ada", 9), ("wout", 0), ("wout", 1), ("ada", 10)]
          + [("wq", 0), ("ada", 11), ("wq", 1), ("wq", 2), ("wq", 3)])
GATE_PIECES = (4, 5, 10, 11)
SLOTS = 4
SLOT_OF = [n % SLOTS for n in range(len(PIECES) - 5)] + [0, 3, 1, 2, 3]
CAND_A = 4 * K
CAND = CAND_A + (K - 4) * 4
LN_EPS = 1e-5
ALPHA = 2.0 ** 0.25
LRU_C = 8.0
DROPPED = -3.0e38
PAD_P = max(WINDOWS)
PAD_C = 4
NT = NK
GT = 2
RT = 2 * GT
OUTS = 2 * TB
TOK = 8
STAGE_T = 64
NST = S // STAGE_T
T_TURN, T_RANK, T_SCATTER, T_STORE = 22, 24, 4 * TB, 8
T_EARLY = T_RANK + T_SCATTER + T_STORE
GATE_UP = 2.0 ** 15

COLS = {}
_n = 0
for _name, _w in (("c", 8), ("ada_b", 48), ("ln0_g", 8), ("ln0_b", 8), ("ln1_g", 8), ("ln1_b", 8),
                  ("pool_scale", 4), ("conv_b", 4), ("lru_ba", 4), ("lru_bx", 4), ("lam", 4),
                  ("conv_w", 16)):
    COLS[_name] = (_n, _n + _w)
    _n += _w
NCOLS = _n
ROWS = ("ln0_g", "ln0_b", "ln1_g", "ln1_b", "ln2_g", "ln2_b", "gate1_b", "gate2_b")
FIN_POOL = 3
BANKS_X = (2, 3, 4, 5)
BANKS_H = (4, 5, 0, 1)
NZ = 12
Y_BANKS = 6
BANKS_RANK = (7, 1)
BANKS_SCATTER = (7, 6)
AT_SCORES = (6, 12)
AT_EXP = 20
C_ID, C_IOTA, C_ONE, C_MEAN, C_EPS, C_CNT = 0, P, 2 * P, 3 * P, 3 * P + 1, 3 * P + 2
NCONST = C_CNT + NG * PAD_P


class Chain:

    def __init__(self, eng, sem, reg=None, per=0):
        self.eng, self.sem, self.reg, self.per, self.n = eng, sem, reg, per, 0

    def link(self, ins):
        ins.then_inc(self.sem, 1)
        self.n += 1
        self.eng.wait_ge(self.sem, self.n if self.reg is None else self.reg * self.per + self.n)


def build(nc, x, cols, rows, consts, ada_w, w_in, w_out, wq, pool_w, wa, wx, k1t, k2t, ut, v, out):
    ctx = ExitStack()
    with ctx:
        def sb(name, shape, dt=F32):
            return ctx.enter_context(nc.sbuf_tensor(name, shape, dt))

        def sem(name):
            return ctx.enter_context(nc.semaphore(name))

        gates = nc.dram_tensor("gates_dram", [NT // 2, P, NST, 2 * STAGE_T], F32, kind="Internal").ap()
        early = nc.dram_tensor("early_dram", [T_EARLY, P, S], F32, kind="Internal").ap()

        bank = [ctx.enter_context(nc.psum_tensor(f"bank{i}", [P, 512], F32)) for i in range(8)]
        xt = sb("xt", [P, TB, D])
        row_g = sb("row_g", [P, D])
        row_b = sb("row_b", [P, D])
        row_gate = sb("row_gate", [P, D])
        cst = sb("cst", [P, NCONST])
        col = sb("col", [P, NCOLS])
        mod = sb("mod", [P, 48])
        sc = sb("sc", [P, 96])
        st = sb("st", [P, TB, 2, 6])
        mv = sb("mv", [P, TB, 2])
        sd = sb("sd", [P, TB])
        rstd = sb("rstd", [P, TB])
        nmean = sb("nmean", [P, TB])
        ramp = sb("ramp", [P, NG, PAD_P])
        hsum = sb("hsum", [P, H, KD])
        hmean = sb("hmean", [P, H, KD])
        h_hi = sb("h_hi", [P, KD, S], F32R)
        before = ExitStack()
        ARENA = 23552
        wbuf = before.enter_context(nc.sbuf_tensor("wbuf", [P, SLOTS * KD * CHUNK_C], F32))
        arena = before.enter_context(nc.sbuf_tensor("arena", [P, ARENA], F32))
        before.close()
        u_raw = sb("u_raw", [P, RT, KD, P])
        v_raw = sb("v_raw", [P, RT, D])
        early_in = sb("early_in", [P, RT, S])
        gate_in = sb("gate_in", [P, 2, NST, 2, STAGE_T])
        acc = sb("acc", [P, TB, D])
        v_hi, v_lo = (sb(n, [P, RT, D], F32R) for n in ("v_hi", "v_lo"))
        w_hi, w_lo = (sb(n, [P, RT, S], F32R) for n in ("w_hi", "w_lo"))
        w_full = sb("w_full", [P, GT, S])
        u_hi, u_lo = (sb(n, [P, GT, KD, P], F32R) for n in ("u_hi", "u_lo"))
        h_lo = sb("h_lo", [P, KD, S], F32R)
        gelu_out = sb("gelu_out", [P, GT, S])

        ident = cst[:, C_ID:C_ID + P]
        iota = cst[:, C_IOTA:C_IOTA + P]
        ones = cst[:, C_ONE:C_ONE + P]
        mean_col = cst[:, C_MEAN:C_MEAN + 1]
        eps = cst[:, C_EPS:C_EPS + 1]
        inv_count = cst[:, C_CNT:C_CNT + NG * PAD_P].rearrange("p (g w) -> p g w", g=NG)

        def vec(name, j=None):
            a, b = COLS[name]
            return col[:, a:b] if j is None else col[:, a + j:a + j + 1]

        silu_c = sc[:, 0:8]
        scale1, bias1, scale2, bias2 = (sc[:, 8 * n:8 * n + 8] for n in (1, 2, 3, 4))
        decay = sc[:, 40:44]
        ndecay = sc[:, 44:48]
        t4 = [sc[:, 48 + 4 * n:52 + 4 * n] for n in range(7)]

        hT = wbuf[:, 3 * KD * CHUNK_C:].rearrange("p (k n) -> p k n", k=KD)
        piece_buf = wbuf[:, :].rearrange("p (s k n) -> p s k n", s=SLOTS, k=KD)

        def carve(spec):
            at, got = 0, []
            for shape in spec:
                n = 1
                for w in shape:
                    n *= w
                a = arena[:, at:at + n]
                if len(shape) == 2:
                    a = a.rearrange("p (a b) -> p a b", a=shape[0])
                if len(shape) == 3:
                    a = a.rearrange("p (a b c) -> p a b c", a=shape[0], b=shape[1])
                got.append(a)
                at += n
            assert at <= ARENA, at
            return got

        AFTER_Z = (8192 + 5120)
        zp, zx, zg, pa, pb, xc, pw = carve(
            [(NG, PAD_P + S), (4, PAD_C + S), (4, S), (NG, PAD_P + S), (NG, PAD_P + S), (4, S), (NG, P)])
        _, yT, gr, gi, wab, wxb = carve([(AFTER_Z,), (KD, S), (4, S), (4, S), (4, P), (4, P)])
        part = arena[:, ARENA - 2 * CHUNK_C:].rearrange("p (b n) -> p b n", b=2)
        (qT, sq, keys, e1, e2, wt, vs, s_all, s_val, s_pos, s_posf, cand, c_val, c_idx, dec, eq_a, eq_b,
         pk) = carve(
            [(2, 2, S), (2, 2, S), (2, NK), (TB, PICKS), (TB, PICKS), (TB, PICKS), (TB, PICKS),
             (2, TB, DK), (2, TB, K), (2, TB, K), (2, TB, K), (TB, CAND), (TB, K), (TB, K), (8, TB * K),
             (TB * K, K), (TB * K, K), (4, TB * H)])
        stage_b, tail = carve([(NT, STAGE_T), (9 * P * TOK // 2 + S,)])
        stage = [wbuf[:, KD * CHUNK_C:3 * KD * CHUNK_C].rearrange("p (a b) -> p a b", a=NT), stage_b]
        onehot_words = 9 * P * TOK // 2
        hot = tail[:, :onehot_words].bitcast(F16).rearrange("p (n i t) -> p n i t", n=9, t=TOK)
        key_of = hot[:, 0]
        onehot = [hot[:, 1 + 2 * b:3 + 2 * b] for b in range(2)]
        gate = [hot[:, 5 + 2 * b:7 + 2 * b] for b in range(2)]
        wT = tail[:, onehot_words:]
        iT, wThl = (arena[:, a:a + S].bitcast(F16).rearrange("p (n t) -> p n t", n=2)
                    for a in (ARENA - 2 * S, ARENA - S))
        i1T, i2T, wTh, wTl = iT[:, 0], iT[:, 1], wThl[:, 0], wThl[:, 1]

        s_x = [sem(f"x_landed{n}") for n in range(TB)]
        s_piece = [sem(f"piece_landed{n}") for n in range(SLOTS)]
        s_u = [sem(f"u_landed{n}") for n in range(RT)]
        s_v = [sem(f"v_landed{n}") for n in range(RT)]
        s_g = [sem(f"gate_pair_landed{n}") for n in range(2)]
        s_early = [sem(f"early_landed{n}") for n in range(RT)]
        s_spill = [sem(f"early_stored{n}") for n in range(GT)]
        s_cst, s_col, s_rows, s_gatew, s_keys, s_out = (
            sem(n) for n in ("cst_landed", "col_landed", "rows_landed", "gatew_landed", "keys_landed",
                             "out_stored"))
        s_stage = [sem(f"stage_stored{n}") for n in range(2)]
        (s_zero, s_silu, s_modmm, s_sc, s_aggr, s_sd, s_ln, s_tr, s_h, s_zmm, s_zev, s_poolmm, s_pooly,
         s_poolev, s_conv, s_gmm, s_sig, s_absl, s_expl, s_decay, s_a, s_th, s_bsq, s_sqrt, s_ix, s_gelu,
         s_lru, s_part, s_gatein, s_rowg, s_ymm, s_yres, s_x0mul, s_x0) = (
            sem(n) for n in (
                "pads_zeroed", "silu_made", "mod_summed", "scales_ready", "stats_ready", "sd_ready",
                "normalised", "transposed", "h_ready", "z_summed", "z_ready", "pool_summed", "pool_input_ready",
                "pool_ready", "conv_ready", "gate_summed", "gate_ready", "abs_lambda_ready", "exp_lambda_ready",
                "decay_ready", "a_ready", "tanh_ready", "b_square_ready", "b_root_ready", "gated_x_ready",
                "gelu_ready", "lru_ready", "mod_part_ready", "gate_bias_landed", "gate_rows_ready", "y_summed", "y_read",
                "residual_scaled", "residual_ready"))
        (s_hmean, s_centre, s_qmm, s_qev, s_smm, s_sev, s_routed, s_e1e2, s_qsd,
         s_shift, s_exp, s_wt, s_hot, s_scmm, s_scev) = (
            sem(n) for n in (
                "head_mean_ready", "wq_centred", "q_summed", "q_ready", "scores_summed", "scores_ready",
                "scores_ranked", "experts_ready",
                "q_sd_ready", "values_shifted", "exp_ready", "weights_ready",
                "onehots_ready", "scatter_bank_full", "scatter_bank_read"))
        s_hhi, s_hlo, s_uhi, s_ulo, s_vhi, s_vlo, s_whi, s_wlo, s_keyof = (
            sem(n) for n in ("h_hi_ready", "h_lo_ready", "u_hi_ready", "u_lo_ready", "v_hi_ready", "v_lo_ready",
                             "weighted_hi_ready", "weighted_lo_ready", "key_table_ready"))
        s_amm, s_act, s_w, s_vmm, s_acc, s_zacc, s_fsd, s_frs, s_fnorm, s_fing = (
            sem(n) for n in ("expert_summed", "expert_gelu", "expert_weighted", "value_summed", "value_added",
                             "acc_zeroed", "final_sd_ready", "final_scale_ready", "final_normalised", "final_times_gain"))
        s_fin = [sem(f"output{n}_ready") for n in range(TB)]
        s_turn = sem("ranking_turn")
        s_wthi, s_wtlo = sem("weights_hi_ready"), sem("weights_lo_ready")
        s_hot0, s_hot1 = sem("first_buffers_onehots_ready"), sem("second_buffers_onehots_ready")
        s_hotlo = sem("low_onehots_ready")
        s_cv, s_cl, s_cs, s_cf, s_ff = (sem(n) for n in ("vector_step", "route_step", "softmax_step",
                                                   "final_step", "final_stats"))

        src = {"ada": ada_w, "win": w_in, "wout": w_out, "wq": wq}
        at_piece = {p: n for n, p in enumerate(PIECES)}
        ada_order = [j for name, j in PIECES if name == "ada"]
        win_order = [j for name, j in PIECES if name == "win"]

        def piece(name, j):
            return piece_buf[:, SLOT_OF[at_piece[(name, j)]]]

        def wait_piece(eng, name, j):
            n = at_piece[(name, j)]
            eng.wait_ge(s_piece[SLOT_OF[n]], 16 * SLOT_OF[:n + 1].count(SLOT_OF[n]))

        def used_up(n):
            name, j = PIECES[n]
            if name == "ada":
                return s_part, ada_order.index(j) + 1
            if name == "win":
                return s_wtlo, 4 * (win_order.index(j) + 1)
            if name == "wout":
                return s_ymm, 2 * TB
            return s_centre, 2 * (j + 1)

        def weights(n):
            if n < NZ:
                return piece("win", win_order[n // 4])[:, :, n % 4 * P:(n % 4 + 1) * P]
            h, half = divmod(n - NZ, 2)
            at = (h % 2) * DK + half * P
            return piece("wq", h // 2)[:, :, at:at + P]

        def both_of(tables, at):
            return tables[:, :, bass.ds(at, TOK)].unsqueeze(2).to_broadcast([P, 2, P, TOK])

        def of(table, at):
            return table[:, bass.ds(at, TOK)].unsqueeze(1).to_broadcast([P, P, TOK])

        block = ctx.enter_context(nc.Block())

        @block.sync
        def _(sp):
            for tb in range(TB):
                sp.dma_start(xt[:, tb, :], x[tb * P:(tb + 1) * P, :]).then_inc(s_x[tb], 16)
            for n, (name, j) in enumerate(PIECES):
                slot = SLOT_OF[n]
                if (name, j) in (("win", 0), ("wq", 3)):
                    sp.wait_ge(s_hlo, KD if name == "win" else 2 * KD)
                if slot in SLOT_OF[:n]:
                    sp.wait_ge(*used_up(max(m for m in range(n) if SLOT_OF[m] == slot)))
                sp.dma_start(piece_buf[:, slot], src[name][j]).then_inc(s_piece[slot], 16)

            def load_u(i, c):
                tile = i * RT + (c + RT)
                sp.wait_ge(s_ulo, i * RT + (c + 1))
                sp.dma_start(u_raw[:, c % RT:c % RT + 1], ut[bass.ds(tile, 1)]
                             .rearrange("a p k n -> p a k n")).then_inc(s_u[c % RT], 16)

            def store_early(i, c):
                tile = i * RT + c
                sp.wait_ge(s_act, i * RT + (c + 1))
                sp.dma_start(early[bass.ds(tile, 1)].rearrange("a p n -> p a n"),
                             gelu_out[:, c % GT:c % GT + 1, :]).then_inc(s_spill[c % GT], 16)

            sp.wait_ge(s_wtlo, NZ + 4)
            for s in range(RT):
                sp.dma_start(u_raw[:, s], ut[s]).then_inc(s_u[s], 16)
            with sp.Fori(0, T_RANK // RT) as i:
                for s in range(RT):
                    load_u(i, s)
                    store_early(i, s)
            with sp.Fori(0, TB) as i:
                for s in range(RT):
                    load_u(i, T_RANK + s)
                    if s % 2:
                        block_of = i * 2 + s // 2
                        sp.wait_ge(s_scev, i * (P // 4) + (4 + (s // 2 + 1) * STAGE_T // 4))
                        sp.dma_start(gates[:, :, bass.ds(block_of, 1), :].rearrange("g p a n -> p g a n"),
                                     stage[s // 2].rearrange("p (g j a) t -> p g a (j t)", j=2, a=1)
                                     ).then_inc(s_stage[s // 2], 16)
                    store_early(i, T_RANK + s)
            sp.wait_ge(s_stage[0], 16 * (TB + 1))
            for s in range(2):
                sp.dma_start(v_raw[:, s, :], v[s]).then_inc(s_v[s], 16)
            for s in range(T_STORE):
                load_u(0, T_RANK + T_SCATTER + s)
                store_early(0, T_RANK + T_SCATTER + s)
                if s < RT:
                    sp.dma_start(early_in[:, s, :], early[s]).then_inc(s_early[s], 16)
                if s == RT - 1:
                    sp.wait_ge(s_stage[1], 16 * (TB + 1))
                    for g in range(2):
                        sp.dma_start(gate_in[:, g], gates[g].rearrange("p b (j t) -> p b j t", j=2)
                                     ).then_inc(s_g[g], 16)
            for s in range(2, RT):
                sp.dma_start(v_raw[:, s, :], v[s]).then_inc(s_v[s], 16)
            for s in range(GT):
                sp.wait_ge(s_spill[s], 16 * T_EARLY // GT)

            def load(i, with_u, with_early):
                for s in range(RT):
                    tile, pair = i * RT + (RT + s), i * 2 + (2 + s // 2)
                    if with_u:
                        load_u(i, s)
                    sp.wait_ge(s_vlo, i * RT + (s + 1))
                    sp.dma_start(v_raw[:, s:s + 1, :], v[bass.ds(tile, 1)].rearrange("a p n -> p a n")
                                 ).then_inc(s_v[s], 16)
                    if with_early or s % 2:
                        sp.wait_ge(s_w, i * RT + (s + 1))
                    if with_early:
                        sp.dma_start(early_in[:, s:s + 1, :],
                                     early[bass.ds(tile, 1)].rearrange("a p n -> p a n")
                                     ).then_inc(s_early[s], 16)
                    if s % 2:
                        g = s // 2
                        sp.dma_start(gate_in[:, g:g + 1].rearrange("p a b j t -> p a (b j t)"),
                                     gates[bass.ds(pair, 1)].rearrange("a p b n -> p a (b n)")
                                     ).then_inc(s_g[g], 16)

            with sp.Fori(0, T_EARLY // RT - 1) as i:
                load(i, False, True)
            load(T_EARLY // RT - 1, False, False)
            with sp.Fori(T_EARLY // RT, NT // RT - 1) as i:
                load(i, True, False)
            for tb in range(TB):
                sp.wait_ge(s_fin[tb], 1)
                sp.dma_start(out[tb * P:(tb + 1) * P, :], xt[:, tb, :]).then_inc(s_out, 16)
            sp.wait_ge(s_out, 16 * TB)

        @block.gpsimd
        def _(pool):
            def load_rows(g, b):
                for row, name in ((row_g, g), (row_b, b)):
                    r = ROWS.index(name)
                    pool.dma_start(row[:, :], rows[r:r + 1, :].to_broadcast([P, D])).then_inc(s_rows, 16)

            def load_gate_bias(name):
                r = ROWS.index(name)
                pool.dma_start(row_gate[:, :], rows[r:r + 1, :].to_broadcast([P, D])).then_inc(s_gatein, 16)

            for buf in (zp[:, :, 0:PAD_P], pa[:, :, 0:PAD_P], pb[:, :, 0:PAD_P], zx[:, :, 0:PAD_C], wab, wxb):
                pool.memset(buf, 0.0).then_inc(s_zero, 1)
            pool.wait_ge(s_zero, 6)
            for dst, w in ((wab, wa), (wxb, wx)):
                for o in range(2):
                    pool.dma_start(dst[64 * o:64 * o + 64, :, 64 * o:64 * o + 64],
                                   w[o::2].rearrange("c i j -> i c j")).then_inc(s_gatew, 16)
            pool.dma_start(pw, pool_w.rearrange("g i j -> i g j")).then_inc(s_gatew, 16)

            def affine(nth, n):
                if n == 0:
                    pool.wait_ge(s_tr, KD * (nth + 1))
                    pool.wait_ge(s_rows, 32 * (nth + 1))
                tb = n % TB
                if n < TB:
                    pool.tensor_tensor(xt[:, tb, :], xt[:, tb, :], row_g[:, :], ALU.mult).then_inc(s_x0mul, 1)
                else:
                    pool.wait_ge(s_x0mul, TB * nth + tb + 1)
                    pool.tensor_tensor(xt[:, tb, :], xt[:, tb, :], row_b[:, :], ALU.add).then_inc(s_x0, 1)

            pool.wait_ge(s_piece[3], 16)
            load_rows("ln0_g", "ln0_b")
            load_gate_bias("gate1_b")
            def lo_weights(n):
                pool.wait_ge(s_wthi, n + 1)
                pool.tensor_tensor(u_lo[:, n % 2], weights(n), u_hi[:, n % 2].bitcast(F32), ALU.subtract
                                   ).then_inc(s_wtlo, 1)

            lo_weights(0)
            lo_weights(1)
            for n in range(2 * TB):
                affine(0, n)
                lo_weights(n + 2)
            for n in range(2 * TB + 2, NZ):
                lo_weights(n)
            pool.wait_ge(s_x0, TB)
            load_rows("ln1_g", "ln1_b")
            pool.wait_ge(s_sig, 8)
            for c in range(4):
                pool.tensor_tensor(gi[:, c, :], gi[:, c, :], xc[:, c, :], ALU.mult).then_inc(s_ix, 1)
            def centre(h):
                pool.wait_ge(s_hmean, h + 1)
                w = piece("wq", h // 2)[:, :, (h % 2) * DK:(h % 2 + 1) * DK]
                pool.tensor_tensor(w, w, hmean[:, h, :].unsqueeze(2).to_broadcast([P, KD, DK]), ALU.add
                                   ).then_inc(s_centre, 1)

            centre(0)
            pool.wait_ge(s_ymm, 2 * TB)
            pool.wait_ge(s_yres, 2 * TB)
            load_gate_bias("gate2_b")

            pool.dma_start(keys[:, 0, :], k1t).then_inc(s_keys, 16)
            pool.dma_start(keys[:, 1, :], k2t).then_inc(s_keys, 16)
            lo_weights(NZ)
            lo_weights(NZ + 1)
            for h in range(1, H):
                centre(h)
                lo_weights(NZ + 2 * h)
                lo_weights(NZ + 2 * h + 1)

            def split_u(i, c):
                pool.wait_ge(s_uhi, i * RT + (c + 1))
                pool.tensor_tensor(u_lo[:, c % GT], u_raw[:, c % RT], u_hi[:, c % GT].bitcast(F32), ALU.subtract
                                   ).then_inc(s_ulo, 1)

            def split_v(s, n):
                pool.wait_ge(s_vhi, n + 1)
                pool.tensor_tensor(v_lo[:, s, :], v_raw[:, s, :], v_hi[:, s, :].bitcast(F32), ALU.subtract
                                   ).then_inc(s_vlo, 1)

            split_u(0, 0)
            split_u(0, 1)
            pool.wait_ge(s_wtlo, NZ + 2 * H)
            pool.memset(acc[:, :, :], 0.0).then_inc(s_zacc, 1)
            for n in range(2 * TB):
                split_u(0, GT + n)
                affine(1, n)
            pool.wait_ge(s_x0, 2 * TB)
            load_rows("ln2_g", "ln2_b")
            with pool.Fori(2 * TB // RT, T_RANK // RT - 1) as i:
                for s in range(RT):
                    split_u(i, GT + s)
            for n in range(T_RANK - RT, T_RANK - 1):
                split_u(0, GT + n)
            with pool.Fori(0, TB) as i:
                for step in range(2 * RT):
                    pool.wait_ge(s_hot1, i * (2 * RT) + (step + 1))
                    pool.tensor_tensor(gate[1][:, 1], onehot[1][:, 0], of(wTl, i * P + (step * 2 + 1) * TOK), ALU.mult
                                       ).then_inc(s_hotlo, 1)
                    if step % 2:
                        split_u(i, T_RANK + GT - 1 + step // 2)
            for n in range(T_EARLY - T_STORE - 1, T_EARLY):
                if n == T_EARLY - GT:
                    for s in range(GT):
                        split_v(s, s)
                split_u(0, GT + n)

            with pool.Fori(0, NT // RT - 1) as i:
                for c in range(GT, GT + RT):
                    split_v(c % RT, i * RT + c)
            for n in range(NT - GT, NT):
                split_v(n % RT, n)
            pool.wait_ge(s_rows, 96)
            for tb in range(FIN_POOL):
                pool.wait_ge(s_fnorm, tb + 1)
                pool.tensor_tensor(xt[:, tb, :], xt[:, tb, :], row_g[:, :], ALU.mult).then_inc(s_fing, 1)
                pool.wait_ge(s_fing, tb + 1)
                pool.tensor_tensor(xt[:, tb, :], xt[:, tb, :], row_b[:, :], ALU.add).then_inc(s_fin[tb], 1)

        @block.scalar
        def _(act):
            act.dma_start(col[:, :], cols).then_inc(s_col, 16)
            act.dma_start(cst[:, :], consts).then_inc(s_cst, 16)
            act.wait_ge(s_col, 16)
            act.wait_ge(s_cst, 16)
            act.activation(silu_c, vec("c"), ACT.Silu).then_inc(s_silu, 1)
            act.wait_ge(s_absl, 1)
            act.activation(t4[2], t4[0], ACT.Exp, scale=-1.0).then_inc(s_expl, 1)

            def root_of_variance(nth):
                for tb in range(TB):
                    act.wait_ge(s_aggr, TB * nth + tb + 1)
                    act.activation(sd[:, tb:tb + 1], mv[:, tb, 1:2], ACT.Sqrt, bias=eps).then_inc(s_sd, 1)

            def modulate(nth, banks, scale, bias):
                act.wait_ge(s_sc, nth + 1)
                for k in range(KD):
                    act.wait_ge(s_tr, KD * nth + k + 1)
                    act.activation(h_hi[:, k, :], bank[banks[k % len(banks)]][:, :], ACT.Identity,
                                   bias=bias[:, k:k + 1], scale=scale[:, k:k + 1]).then_inc(s_hhi, 1)

            def hi_weights(n):
                if n < NZ:
                    wait_piece(act, "win", win_order[n // 4])
                    if n >= 2:
                        act.wait_ge(s_zmm, n - 1)
                else:
                    m = n - NZ
                    act.wait_ge(s_centre, m // 2 + 1)
                    if m >= 2:
                        act.wait_ge(s_qmm, m - 1)
                act.activation(u_hi[:, n % 2], weights(n), ACT.Copy).then_inc(s_wthi, 1)

            root_of_variance(0)
            hi_weights(0)
            modulate(0, BANKS_X, scale1, bias1)
            hi_weights(1)
            act.wait_ge(s_zero, 4)
            for n in range(12):
                dst = (zx[:, n % 4, PAD_C:], zp[:, n % 4, PAD_P:], zg[:, n % 4, :])[n // 4]
                act.wait_ge(s_zmm, n + 1)
                act.activation(dst, bank[n % 2][:, :], ACT.Copy).then_inc(s_zev, 1)
                if n + 2 < NZ:
                    hi_weights(n + 2)
            act.wait_ge(s_zev, 12)
            for c in range(4):
                act.activation(zg[:, c, :], zg[:, c, :], ACT.Gelu_apprx_tanh).then_inc(s_gelu, 1)
            for n in range(8):
                c, dst, bias = n // 2, (gr, gi)[n % 2], ("lru_ba", "lru_bx")[n % 2]
                act.wait_ge(s_gmm, n + 1)
                act.activation(dst[:, c, :], bank[4 + n % 2][:, :], ACT.Sigmoid, bias=vec(bias, c)).then_inc(s_sig, 1)
            for g in range(NG):
                act.wait_ge(s_poolmm, g + 1)
                act.activation(yT[:, g, :], bank[(6, 0)[g % 2]][:, :], ACT.Copy, scale=vec("pool_scale", g)
                               ).then_inc(s_poolev, 1)
            act.wait_ge(s_decay, 1)
            act.wait_ge(s_sig, 8)
            for c in range(4):
                act.activation(pa[:, c, PAD_P:], gr[:, c, :], ACT.Exp, scale=decay[:, c:c + 1]).then_inc(s_a, 1)
            act.wait_ge(s_a, 4)
            for c in range(4):
                act.activation(gr[:, c, :], gr[:, c, :], ACT.Tanh, scale=ndecay[:, c:c + 1]).then_inc(s_th, 1)
            for c in range(4):
                act.wait_ge(s_bsq, c + 1)
                act.activation(pb[:, c, PAD_P:], pb[:, c, PAD_P:], ACT.Sqrt).then_inc(s_sqrt, 1)
            root_of_variance(1)
            def queries(i, par, h, first):
                if not first:
                    act.wait_ge(s_smm, h - 1)
                for half in range(2):
                    act.wait_ge(s_qmm, h * 2 + (half + 1))
                    act.activation(qT[:, par, half, :], bank[half][:, :], ACT.Copy)
                    act.activation(sq[:, par, half, :], bank[half][:, :], ACT.Square).then_inc(s_qev, 1)
                    if h + 1 < H:
                        hi_weights(NZ + 2 * h + 2 + half)

            act.wait_ge(s_ymm, 2 * TB)
            hi_weights(NZ)
            hi_weights(NZ + 1)
            modulate(1, BANKS_H, scale2, bias2)

            def scores(par, h, first):
                act.wait_ge(s_smm, h + 1)
                if not first:
                    act.wait_ge(s_routed, h - 1)
                for b in range(2):
                    act.activation(s_all[:, par, 2 * b:2 * b + 2, :],
                                   bank[(2, 5)[par] + b][:, :].rearrange("p (t n) -> p t n", t=2), ACT.Copy
                                   ).then_inc(s_sev, 1)

            def hi_u(i, c):
                act.wait_ge(s_u[c % RT], i * 16 + 16 * (c // RT + 1))
                if c >= GT or not isinstance(i, int):
                    act.wait_ge(s_amm, i * RT + (c - (GT - 1)))
                act.activation(u_hi[:, c % GT], u_raw[:, c % RT], ACT.Copy).then_inc(s_uhi, 1)

            def early_gelu(i, c, banks):
                act.wait_ge(s_amm, i * RT + (c + 1))
                if c >= GT or not isinstance(i, int):
                    act.wait_ge(s_spill[c % GT], i * 32 + 16 * (c // GT))
                act.activation(gelu_out[:, c % GT, :], bank[banks[c % GT]][:, :], ACT.Gelu_apprx_tanh
                               ).then_inc(s_act, 1)
                hi_u(i, c + GT)

            def rank_tiles(a, b):
                for n in range(a, b):
                    early_gelu(0, n, BANKS_RANK)

            queries(0, 0, 0, True)
            queries(0, 1, 1, True)
            scores(0, 0, True)
            for h in range(2, H):
                queries(0, h % 2, h, False)
                behind = 1 if h < H // 2 else 2
                if h not in (H // 2, H - 1):
                    scores((h - behind) % 2, h - behind, h - behind < 2)
            hi_u(0, 0)
            hi_u(0, 1)
            scores(1, H - 3, False)
            rank_tiles(0, AT_SCORES[0])
            scores(0, H - 2, False)
            rank_tiles(AT_SCORES[0], AT_SCORES[1])
            scores(1, H - 1, False)
            act.activation(pk[:, 0, :], bank[4][:, 0:TB * H], ACT.Sqrt, bias=eps).then_inc(s_qsd, 1)
            rank_tiles(AT_SCORES[1], AT_EXP)
            act.wait_ge(s_shift, 1)
            act.activation(vs, wt, ACT.Exp).then_inc(s_exp, 1)
            rank_tiles(AT_EXP, T_TURN)
            for n, (dst, scale) in enumerate(((i1T, 1.0), (i2T, 1.0), (wT[:, 0:S // 2], GATE_UP),
                                              (wT[:, S // 2:], GATE_UP))):
                act.wait_ge(s_scmm, n + 1)
                src_at = slice(0, S) if n < 2 else slice((n - 2) * S // 2, (n - 1) * S // 2)
                act.activation(dst, bank[n][:, src_at], ACT.Copy, scale=scale).then_inc(s_scev, 1)
            for n in range(T_TURN, T_RANK):
                early_gelu(0, n, BANKS_SCATTER)
            with act.Fori(0, TB) as i:
                for s in range(RT):
                    b = s // 2
                    if s % 2 == 0:
                        act.wait_ge(s_stage[b], i * 16 + 16)
                    for q in range(8):
                        act.wait_ge(s_scmm, i * (P // 4) + (4 + s * 8 + q + 1))
                        at = (s % 2) * 32 + 4 * q
                        dst = stage[b][:, :, at:at + 4].rearrange("p i t -> p t i")
                        act.activation(dst, bank[q % 4][:, :].rearrange("p (t i) -> p t i", t=4), ACT.Copy,
                                       scale=1.0 / GATE_UP).then_inc(s_scev, 1)
                    early_gelu(i, T_RANK + s, BANKS_SCATTER)
            def hi_v(s, landed, free):
                act.wait_ge(s_v[s], landed)
                if free is not None:
                    act.wait_ge(s_vmm, free)
                act.activation(v_hi[:, s, :], v_raw[:, s, :], ACT.Copy).then_inc(s_vhi, 1)

            for n in range(T_STORE):
                early_gelu(0, T_RANK + T_SCATTER + n, BANKS_SCATTER)
                if n == T_STORE - 3:
                    act.wait_ge(s_stage[1], 16 * (TB + 1))
                    for j in range(GT):
                        hi_v(j, 16, None)

            def gelu(i, c, first):
                act.wait_ge(s_amm, i * RT + (c + 1))
                if first:
                    act.wait_ge(s_spill[c % GT], 16 * T_EARLY // GT)
                else:
                    act.wait_ge(s_w, i * RT + (c - (GT - 1)))
                act.activation(gelu_out[:, c % GT, :], bank[c % RT][:, :], ACT.Gelu_apprx_tanh).then_inc(s_act, 1)

            def group(i, g2, first, with_inputs, ahead, last):
                g = i * 2 + g2
                if last:
                    return
                for j in range(GT):
                    c = (g2 + 1) * GT + j
                    hi_v(c % RT, i * 16 + 16 * (c // RT + 1), None if first else g * OUTS)
                for j in range(GT):
                    c = (g2 + 1) * GT + j
                    if with_inputs:
                        gelu(i, c, isinstance(i, int) and i * RT + c < T_EARLY + GT)
                    if with_inputs and ahead:
                        hi_u(i, c + GT)

            group(0, 0, True, False, False, False)
            group(0, 1, False, False, False, False)
            with act.Fori(1, T_EARLY // RT - 1) as i:
                group(i, 0, False, False, False, False)
                group(i, 1, False, False, False, False)
            group(T_EARLY // RT - 1, 0, False, False, False, False)
            group(T_EARLY // RT - 1, 1, False, True, True, False)
            with act.Fori(T_EARLY // RT, NT // RT - 1) as i:
                group(i, 0, False, True, True, False)
                group(i, 1, False, True, True, False)
            group(NT // RT - 1, 0, False, True, False, False)
            for tb in range(TB):
                act.wait_ge(s_ff, tb + 1)
                act.activation(sd[:, tb:tb + 1], mv[:, tb, 1:2], ACT.Sqrt, bias=eps).then_inc(s_fsd, 1)
                act.wait_ge(s_frs, tb + 1)
                act.activation(xt[:, tb, :], xt[:, tb, :], ACT.Identity, bias=nmean[:, tb:tb + 1],
                               scale=rstd[:, tb:tb + 1]).then_inc(s_fnorm, 1)

        @block.tensor
        def _(pe):
            def modulation(j):
                n = ada_order.index(j)
                pe.wait_ge(s_part, n + 1)
                if j in GATE_PIECES:
                    mm = pe.matmul(bank[(6, 3)[j % 2]][:, :], ones, part[:, n % 2, :], start=True, stop=True)
                else:
                    for m in range(4):
                        mm = pe.matmul(bank[7][:, 4 * j + m:4 * j + m + 1], part[:, n % 2, m * P:(m + 1) * P],
                                       ones[:, 0:1], start=True, stop=True)
                mm.then_inc(s_modmm, 1)

            def transposes(nth, banks, chunks=range(KD)):
                pe.wait_ge(s_ln, TB * (nth + 1))
                for k in chunks:
                    if k >= len(banks):
                        pe.wait_ge(s_h, KD * nth + k - len(banks) + 1)
                    for tb in range(TB):
                        mm = pe.transpose(bank[banks[k % len(banks)]][:, tb * P:(tb + 1) * P],
                                          xt[:, tb, k * P:(k + 1) * P], ident)
                    mm.then_inc(s_tr, 1)

            def thrice(out, k, n, pairs):
                (a_hi, a_lo), (b_hi, b_lo) = pairs
                pe.matmul(out, a_hi, b_hi, start=(k == 0), stop=False)
                pe.matmul(out, a_hi, b_lo, start=False, stop=False)
                return pe.matmul(out, a_lo, b_hi, start=False, stop=(k == n - 1))

            pe.wait_ge(s_cst, 16)
            transposes(0, BANKS_X, range(4))
            for j in range(4):
                modulation(j)
            transposes(0, BANKS_X, range(4, KD))
            for n in range(12):
                pe.wait_ge(s_wtlo, n + 1)
                if n >= 2:
                    pe.wait_ge(s_zev, n - 1)
                for k in range(KD):
                    if n == 0:
                        pe.wait_ge(s_hlo, k + 1)
                    mm = thrice(bank[n % 2][:, :], k, KD, ((u_hi[:, n % 2, k, :], u_lo[:, n % 2, k, :]),
                                                           (h_hi[:, k, :], h_lo[:, k, :])))
                mm.then_inc(s_zmm, 1)
                if n % 4 == 3:
                    modulation(4 + n // 2 - 1)
                    modulation(4 + n // 2)
            pe.wait_ge(s_gatew, 80)
            for n in range(8):
                c = n // 2
                pe.wait_ge(s_conv, c + 1)
                if n >= 2:
                    pe.wait_ge(s_sig, n - 1)
                pe.matmul(bank[4 + n % 2][:, :], (wab, wxb)[n % 2][:, c, :], xc[:, c, :], start=True, stop=True
                          ).then_inc(s_gmm, 1)
            pe.wait_ge(s_zev, 12)
            pe.wait_ge(s_rowg, 2)
            for g in range(NG):
                pe.wait_ge(s_pooly, g + 1)
                if g >= 2:
                    pe.wait_ge(s_poolev, g - 1)
                pe.matmul(bank[(6, 0)[g % 2]][:, :], pw[:, g, :], (pa, pb)[g % 2][:, g, PAD_P:],
                          start=True, stop=True).then_inc(s_poolmm, 1)
            pe.wait_ge(s_poolev, NG)
            pe.wait_ge(s_sig, 8)
            wait_piece(pe, "wout", 0)
            wait_piece(pe, "wout", 1)

            def mixer_output(n, chunks):
                for k in chunks:
                    mm = pe.matmul(bank[n % Y_BANKS][:, :], yT[:, k, (n // 2) * P:(n // 2 + 1) * P],
                                   piece("wout", n % 2)[:, k, :], start=(k == 0), stop=(k == KD - 1))
                return mm

            for n in range(Y_BANKS):
                mixer_output(n, range(NG))
            pe.wait_ge(s_lru, 4)
            for n in range(2 * TB):
                if n >= Y_BANKS:
                    pe.wait_ge(s_yres, n - Y_BANKS + 1)
                mixer_output(n, range(NG if n < Y_BANKS else 0, KD)).then_inc(s_ymm, 1)
            transposes(1, BANKS_H)
            pe.wait_ge(s_yres, 2 * TB)
            modulation(10)
            modulation(11)

            def queries(par, h, first):
                for half in range(2):
                    pe.wait_ge(s_wtlo, NZ + 2 * h + half + 1)
                    if not first:
                        pe.wait_ge(s_qev, h * 2 + (half - 1))
                    for k in range(KD):
                        if first:
                            pe.wait_ge(s_hlo, KD + k + 1)
                        mm = thrice(bank[half][:, :], k, KD, ((u_hi[:, half, k, :], u_lo[:, half, k, :]),
                                                              (h_hi[:, k, :], h_lo[:, k, :])))
                    mm.then_inc(s_qmm, 1)

            def scores(par, h, first, var_at):
                pe.wait_ge(s_qev, h * 2 + 2)
                if not first:
                    pe.wait_ge(s_sev, h * 2 - 2)
                for tb in range(TB):
                    for half in range(2):
                        at = (tb % 2) * DK + half * NK
                        pe.matmul(bank[(2, 5)[par] + tb // 2][:, at:at + NK],
                                  qT[:, par, half, tb * P:(tb + 1) * P], keys[:, half, :], start=True, stop=True)
                for tb in range(TB):
                    for half in range(2):
                        mm = pe.matmul(bank[4][:, var_at(tb)], sq[:, par, half, tb * P:(tb + 1) * P], mean_col,
                                       start=(half == 0), stop=(half == 1))
                mm.then_inc(s_smm, 1)

            def static_at(h):
                return lambda tb: slice(h * TB + tb, h * TB + tb + 1)

            pe.wait_ge(s_h, 2 * KD)
            pe.wait_ge(s_yres, 2 * TB)
            queries(0, 0, True)
            queries(1, 1, False)
            pe.wait_ge(s_keys, 32)
            pe.wait_ge(s_rowg, 4)
            scores(0, 0, True, static_at(0))
            queries(0, 2, False)
            scores(1, 1, True, static_at(1))
            for i in range(1, H // 2 - 1):
                queries(1, i * 2 + 1, False)
                scores(0, i * 2, False, static_at(i * 2))
                queries(0, i * 2 + 2, False)
                scores(1, i * 2 + 1, False, static_at(i * 2 + 1))
            queries(1, H - 1, False)
            scores(0, H - 2, False, static_at(H - 2))
            def expert_inputs(i, c, b, free, chunks=range(KD)):
                if 0 in chunks:
                    pe.wait_ge(s_ulo, i * RT + (c + 1))
                    if free is not None:
                        pe.wait_ge(s_act, free)
                for k in chunks:
                    mm = thrice(bank[b][:, :], k, KD, ((u_hi[:, c % GT, k, :], u_lo[:, c % GT, k, :]),
                                                       (h_hi[:, k, :], h_lo[:, k, :])))
                if KD - 1 in chunks:
                    mm.then_inc(s_amm, 1)

            pe.wait_ge(s_qev, 2 * H)
            for c in range(RT):
                if c == GT:
                    scores(1, H - 1, False, static_at(H - 1))
                expert_inputs(0, c, BANKS_RANK[c % GT], c - (GT - 1) if c >= GT else None)
            with pe.Fori(1, T_TURN // RT) as i:
                for c in range(RT):
                    expert_inputs(i, c, BANKS_RANK[c % GT], i * RT + (c - (GT - 1)))
            for c in range(T_TURN // RT * RT, T_TURN):
                expert_inputs(0, c, BANKS_RANK[c % GT], c - (GT - 1))
            pe.wait_ge(s_sev, 2 * H)
            pe.wait_ge(s_wt, 1)
            pe.wait_ge(s_e1e2, H)
            for n, (m, blocks) in enumerate(((e1, range(TB)), (e2, range(TB)), (wt, range(TB // 2)),
                                             (wt, range(TB // 2, TB)))):
                if n == 1:
                    pe.wait_ge(s_act, T_TURN)
                for tb in blocks:
                    mm = pe.transpose(bank[n][:, tb * P:(tb + 1) * P], m[:, tb, :], ident)
                mm.then_inc(s_scmm, 1)

            def scatter(i, step):
                for q in range(4):
                    pe.wait_ge(s_hot, i * (P // TOK) + (step * 2 + q // 2 + 1))
                    if q == 2:
                        pe.wait_ge(s_hotlo, i * (2 * RT) + (step + 1))
                    pe.wait_ge(s_scev, i * (P // 4) + (step * 4 + q + 1))
                    for t in range(4):
                        at, b = 4 * (q % 2) + t, q // 2
                        pe.matmul(bank[q][:, t * P:(t + 1) * P], onehot[b][:, 1, :, at], gate[b][:, 0, :, at],
                                  start=True, stop=False)
                        mm = pe.matmul(bank[q][:, t * P:(t + 1) * P], onehot[b][:, 1, :, at], gate[b][:, 1, :, at],
                                       start=False, stop=True)
                    mm.then_inc(s_scmm, 1)

            for c in range(T_TURN, T_RANK):
                expert_inputs(0, c, BANKS_SCATTER[c % GT], c - (GT - 1))
            with pe.Fori(0, TB) as i:
                for step in range(2 * RT):
                    scatter(i, step)
                    c = T_RANK + step // 2
                    expert_inputs(i, c, BANKS_SCATTER[c % GT], i * RT + (c - (GT - 1)),
                                  range((step % 2) * KD // 2, (step % 2 + 1) * KD // 2))
            for c in range(T_RANK + T_SCATTER, T_EARLY):
                expert_inputs(0, c, BANKS_SCATTER[c % GT], c - (GT - 1))

            def values(o, n, first, slots, j0=0, total=GT):
                t, d = slice(o // 2 * P, (o // 2 + 1) * P), slice(o % 2 * 512, (o % 2 + 1) * 512)
                if not first:
                    pe.wait_ge(s_acc, n - 3)
                for j, s in enumerate(slots, j0):
                    mm = thrice(bank[4 + o % 4][:, :], j, total, ((w_hi[:, s, t], w_lo[:, s, t]),
                                                                       (v_hi[:, s, d], v_lo[:, s, d])))
                if j == total - 1:
                    mm.then_inc(s_vmm, 1)

            def group(i, g2, first, with_inputs):
                g = i * 2 + g2
                for j in range(GT):
                    if with_inputs:
                        c = (g2 + 1) * GT + j
                        expert_inputs(i, c, c % RT, i * RT + (c - (RT - 1)))
                    if j == 0:
                        pe.wait_ge(s_wlo, g * GT + GT)
                        pe.wait_ge(s_vlo, g * GT + GT)
                    for o in range(j * OUTS // GT, (j + 1) * OUTS // GT):
                        if first and o == 2:
                            pe.wait_ge(s_act, T_EARLY)
                        values(o, g * OUTS + o, first and o < 4, range(GT * g2, GT * g2 + GT))

            group(0, 0, True, False)
            group(0, 1, False, False)
            with pe.Fori(1, T_EARLY // RT - 1) as i:
                group(i, 0, False, False)
                group(i, 1, False, False)
            group(T_EARLY // RT - 1, 0, False, False)
            pe.wait_ge(s_scev, 4 + S // 4)
            group(T_EARLY // RT - 1, 1, False, True)
            with pe.Fori(T_EARLY // RT, NT // RT - 1) as i:
                group(i, 0, False, True)
                group(i, 1, False, True)
            for c in range(GT, RT):
                expert_inputs(NT // RT - 1, c, c, NT - RT + (c - (RT - 1)))
            last = (NT // GT - 2) * OUTS
            pe.wait_ge(s_wlo, NT - GT)
            pe.wait_ge(s_vlo, NT - GT)
            for o in range(OUTS // 2):
                values(o, last + o, False, range(GT), 0, RT)
            pe.wait_ge(s_wlo, NT)
            pe.wait_ge(s_vlo, NT)
            for o in range(OUTS // 2):
                values(o, last + o, True, range(GT, RT), GT, RT)
            for o in range(OUTS // 2, OUTS):
                values(o, last + o, False, range(RT), 0, RT)

        @block.vector
        def _(ve):
            steps = Chain(ve, s_cv)
            link = steps.link

            def block_stats(tb):
                for b in range(2):
                    last = ve.bn_stats(st[:, tb, b, :], xt[:, tb, b * 512:(b + 1) * 512])
                link(last)
                ve.bn_aggr(mv[:, tb, :], st[:, tb, :, :]).then_inc(s_aggr, 1)

            def normalise(nth, tb):
                ve.wait_ge(s_sd, TB * nth + tb + 1)
                link(ve.reciprocal(rstd[:, tb:tb + 1], sd[:, tb:tb + 1]))
                ve.wait_ge(s_aggr, TB * nth + tb + 1)
                ve.tensor_scalar(xt[:, tb, :], xt[:, tb, :], mv[:, tb, 0:1], rstd[:, tb:tb + 1],
                                 ALU.subtract, ALU.mult).then_inc(s_ln, 1)

            def partial_modulation(j):
                n = ada_order.index(j)
                wait_piece(ve, "ada", j)
                if n >= 2:
                    ve.wait_ge(s_modmm, n - 1)
                for k in range(KD):
                    if k == 0:
                        link(ve.tensor_scalar(part[:, n % 2, :], piece("ada", j)[:, k, :], silu_c[:, k:k + 1],
                                              None, ALU.mult))
                        continue
                    last = ve.scalar_tensor_tensor(out=part[:, n % 2, :], in0=piece("ada", j)[:, k, :],
                                                   scalar=silu_c[:, k:k + 1], in1=part[:, n % 2, :],
                                                   op0=ALU.mult, op1=ALU.add)
                    if k < KD - 1:
                        link(last)
                last.then_inc(s_part, 1)

            def add_gate_row(nth):
                ve.wait_ge(s_gatein, 16 * (nth + 1))
                for b in range(2):
                    ve.wait_ge(s_modmm, ada_order.index(GATE_PIECES[2 * nth + b]) + 1)
                    part_row = row_gate[:, b * 512:(b + 1) * 512]
                    ve.tensor_tensor(part_row, part_row, bank[(6, 3)[b]][:, :], ALU.add).then_inc(s_rowg, 1)

            def read_mod(a, b, pieces):
                ve.wait_ge(s_modmm, pieces)
                o = COLS["ada_b"][0]
                link(ve.tensor_tensor(mod[:, a:b], bank[7][:, a:b], col[:, o + a:o + b], ALU.add))

            def scales(shift, scale, g, b, out_scale, out_bias):
                ve.scalar_tensor_tensor(out=out_scale, in0=mod[:, scale:scale + 8], scalar=1.0, in1=vec(g),
                                        op0=ALU.add, op1=ALU.mult)
                link(ve.scalar_tensor_tensor(out=out_bias, in0=mod[:, scale:scale + 8], scalar=1.0, in1=vec(b),
                                             op0=ALU.add, op1=ALU.mult))
                ve.tensor_tensor(out_bias, out_bias, mod[:, shift:shift + 8], ALU.add).then_inc(s_sc, 1)

            def low_input(nth, banks, scale, bias):
                ve.wait_ge(s_part, len(ada_order) if nth else 4)
                ve.wait_ge(s_sc, nth + 1)
                for k in range(KD):
                    ve.wait_ge(s_hhi, KD * nth + k + 1)
                    ve.tensor_scalar(hT[:, k, :], bank[banks[k % len(banks)]][:, :], scale[:, k:k + 1],
                                     bias[:, k:k + 1], ALU.mult, ALU.add).then_inc(s_h, 1)
                    ve.wait_ge(s_h, KD * nth + k + 1)
                    ve.tensor_tensor(h_lo[:, k, :], hT[:, k, :], h_hi[:, k, :].bitcast(F32), ALU.subtract
                                     ).then_inc(s_hlo, 1)

            ve.wait_ge(s_col, 16)
            lam, (al, m, e, r, z, z2, p) = vec("lam"), t4
            ve.tensor_scalar(m, lam, -1.0, 0.0, ALU.mult, ALU.max)
            ve.scalar_tensor_tensor(out=al, in0=lam, scalar=-1.0, in1=lam, op0=ALU.mult, op1=ALU.max
                                    ).then_inc(s_absl, 1)
            for tb in range(TB):
                ve.wait_ge(s_x[tb], 16)
                block_stats(tb)
            for tb in range(TB):
                normalise(0, tb)
            ve.wait_ge(s_silu, 1)
            for j in range(4):
                partial_modulation(j)
            read_mod(0, 16, 4)
            scales(0, 8, "ln0_g", "ln0_b", scale1, bias1)
            low_input(0, BANKS_X, scale1, bias1)
            partial_modulation(4)
            partial_modulation(5)
            ve.wait_ge(s_expl, 1)
            link(ve.tensor_scalar(z, e, 2.0, None, ALU.add))
            link(ve.reciprocal(r, z))
            link(ve.tensor_tensor(z, e, r, ALU.mult))
            link(ve.tensor_tensor(z2, z, z, ALU.mult))
            link(ve.tensor_scalar(p, z2, 1.0 / 19, None, ALU.mult))
            for n in range(17, 1, -2):
                link(ve.scalar_tensor_tensor(out=p, in0=p, scalar=1.0 / n, in1=z2, op0=ALU.add, op1=ALU.mult))
            link(ve.scalar_tensor_tensor(out=p, in0=p, scalar=1.0, in1=z, op0=ALU.add, op1=ALU.mult))
            link(ve.scalar_tensor_tensor(out=p, in0=p, scalar=2.0, in1=m, op0=ALU.mult, op1=ALU.add))
            ve.tensor_scalar(decay, p, -LRU_C, None, ALU.mult)
            ve.tensor_scalar(ndecay, p, LRU_C, None, ALU.mult).then_inc(s_decay, 1)

            ve.wait_ge(s_zero, 6)
            for t in range(CONV_W):
                for c in range(4):
                    w = vec("conv_w", 4 * t + c)
                    shifted = zx[:, c, PAD_C - CONV_W + 1 + t:PAD_C - CONV_W + 1 + t + S]
                    if t == 0:
                        ve.wait_ge(s_zev, c + 1)
                        last = ve.tensor_scalar(xc[:, c, :], shifted, w, vec("conv_b", c), ALU.mult, ALU.add)
                    else:
                        last = ve.scalar_tensor_tensor(out=xc[:, c, :], in0=shifted, scalar=w, in1=xc[:, c, :],
                                                       op0=ALU.mult, op1=ALU.add)
                    if t == CONV_W - 1:
                        last.then_inc(s_conv, 1)
                if t < CONV_W - 1:
                    link(last)
            add_gate_row(0)
            partial_modulation(6)
            partial_modulation(7)
            ve.wait_ge(s_zev, 8)
            bufs = (zp, pa, pb, pa, pb)
            for n, w in enumerate(WINDOWS):
                a, b = bufs[n], bufs[n + 1]
                link(ve.tensor_tensor(b[:, n:, PAD_P:], a[:, n:, PAD_P:], a[:, n:, PAD_P - w // 2:PAD_P - w // 2 + S],
                                      ALU.add))
            for g, w in enumerate(WINDOWS):
                last = ve.tensor_tensor(ramp[:, g, :], bufs[g + 1][:, g, PAD_P:2 * PAD_P], inv_count[:, g, :], ALU.mult)
            link(last)
            for g, w in enumerate(WINDOWS):
                b = bufs[g + 1][:, g, PAD_P:]
                last = ve.scalar_tensor_tensor(out=b, in0=b, scalar=1.0 / w, in1=zp[:, g, PAD_P:],
                                               op0=ALU.mult, op1=ALU.subtract)
            link(last)
            for g in range(NG):
                ve.tensor_tensor(bufs[g + 1][:, g, PAD_P:2 * PAD_P], ramp[:, g, :], zp[:, g, PAD_P:2 * PAD_P],
                                 ALU.subtract).then_inc(s_pooly, 1)
            partial_modulation(8)
            partial_modulation(9)
            ve.wait_ge(s_poolmm, NG)
            for c in range(4):
                ve.wait_ge(s_a, c + 1)
                last = ve.tensor_tensor(pb[:, c, PAD_P:], pa[:, c, PAD_P:], pa[:, c, PAD_P:], ALU.mult)
            link(last)
            for c in range(4):
                ve.wait_ge(s_th, c + 1)
                ve.scalar_tensor_tensor(out=pb[:, c, PAD_P:], in0=pb[:, c, PAD_P:], scalar=1.0, in1=gr[:, c, :],
                                        op0=ALU.add, op1=ALU.mult).then_inc(s_bsq, 1)
            for c in range(4):
                ve.wait_ge(s_sqrt, c + 1)
                ve.wait_ge(s_ix, c + 1)
                last = ve.tensor_tensor(pb[:, c, PAD_P:], pb[:, c, PAD_P:], gi[:, c, :], ALU.mult)
            link(last)
            ve.wait_ge(s_ix, 4)
            for c in range(4):
                last = ve.tensor_tensor_scan(xc[:, c, :], pa[:, c, PAD_P:], pb[:, c, PAD_P:], 0.0, ALU.mult, ALU.add)
            link(last)
            ve.wait_ge(s_gelu, 4)
            for c in range(4):
                ve.tensor_tensor(yT[:, NG + c, :], xc[:, c, :], zg[:, c, :], ALU.mult).then_inc(s_lru, 1)
            read_mod(24, 40, 10)
            scales(24, 32, "ln1_g", "ln1_b", scale2, bias2)
            def head_means(i):
                for par in range(2):
                    w = piece_buf[:, bass.ds(i, 1), :, par * DK:(par + 1) * DK]
                    last = ve.tensor_reduce(hsum[:, bass.ds(i * 2 + par, 1), :], w, AX.X, ALU.add)
                return last

            def scaled_means(i):
                ve.tensor_scalar(hmean[:, bass.ds(i * 2, 1), :], hsum[:, bass.ds(i * 2, 1), :],
                                 -1.0 / DK, None, ALU.mult).then_inc(s_hmean, 1)
                ve.tensor_scalar(hmean[:, bass.ds(i * 2 + 1, 1), :], hsum[:, bass.ds(i * 2 + 1, 1), :],
                                 -1.0 / DK, None, ALU.mult).then_inc(s_hmean, 1)

            ve.wait_ge(s_rowg, 2)
            ve.wait_ge(s_x0, TB)
            ve.wait_ge(s_lru, 4)
            partial_modulation(10)
            for tb in range(TB):
                for half in range(2):
                    n = 2 * tb + half
                    ve.wait_ge(s_ymm, n + 1)
                    ve.tensor_tensor(zg[:, n % 4, :], bank[n % Y_BANKS][:, :], row_gate[:, half * 512:(half + 1) * 512],
                                     ALU.mult).then_inc(s_yres, 1)
                ve.wait_ge(s_yres, 2 * tb + 2)
                for half in range(2):
                    piece_x = xt[:, tb, half * 512:(half + 1) * 512]
                    last = ve.scalar_tensor_tensor(out=piece_x, in0=piece_x, scalar=ALPHA,
                                                   in1=zg[:, (2 * tb + half) % 4, :], op0=ALU.mult, op1=ALU.add)
                link(last)
                block_stats(tb)
                if tb:
                    normalise(1, tb - 1)
                else:
                    partial_modulation(11)
                    wait_piece(ve, "wq", 0)
                    link(head_means(0))
                    scaled_means(0)
            normalise(1, TB - 1)

            def top_k(parts, step, done=None):
                for val, idx, data in parts:
                    last = ve.max(val[:, 0:8], data)
                step(last)
                for val, idx, data in parts:
                    ve.max_index(idx[:, 0:8], val[:, 0:8], data)
                for val, idx, data in parts:
                    last = ve.match_replace(data, val[:, 0:8], data, DROPPED)
                step(last)
                for val, idx, data in parts:
                    last = ve.max(val[:, 8:16], data)
                step(last)
                for val, idx, data in parts:
                    last = ve.max_index(idx[:, 8:16], val[:, 8:16], data)
                return last

            ci = c_idx.rearrange("p t k -> p (t k)").bitcast(U32)
            dci = [dec[:, n, :].bitcast(U32) for n in range(4)]
            ka, kb, low = dec[:, 4, :], dec[:, 5, :], dec[:, 6, :]
            iota16 = iota[:, 0:K].unsqueeze(1).to_broadcast([P, TB * K, K])

            def route(par, h, chain):
                def step(ins):
                    chain.link(ins)
                    ve.sem_inc(s_turn, 1)

                ve.wait_ge(s_sev, h * 2 + 2)
                ve.sem_inc(s_turn, 1)
                last = top_k([(s_val[:, half, tb, :], s_pos[:, half, tb, :].bitcast(U32),
                               s_all[:, par, tb, half * NK:(half + 1) * NK])
                              for tb in range(TB) for half in range(2)], step)
                last.then_inc(s_routed, 1)
                ve.wait_ge(s_routed, h + 1)
                ve.tensor_copy(s_posf, s_pos.bitcast(U32))
                ve.tensor_tensor(cand[:, :, 0:CAND_A].rearrange("p t (a b) -> p t a b", a=4),
                                 s_val[:, 0, :, 0:4].unsqueeze(3).to_broadcast([P, TB, 4, K]),
                                 s_val[:, 1, :, :].unsqueeze(2).to_broadcast([P, TB, 4, K]), ALU.add)
                step(ve.tensor_tensor(cand[:, :, CAND_A:].rearrange("p t (a b) -> p t a b", a=K - 4),
                                      s_val[:, 0, :, 4:].unsqueeze(3).to_broadcast([P, TB, K - 4, 4]),
                                      s_val[:, 1, :, 0:4].unsqueeze(2).to_broadcast([P, TB, K - 4, 4]), ALU.add))
                step(top_k([(c_val[:, tb, :], c_idx[:, tb, :].bitcast(U32), cand[:, tb, :]) for tb in range(TB)], step))
                ve.tensor_copy(vs[:, :, bass.ds(h * K, K)], c_val)
                ve.tensor_scalar(dci[0], ci, 2, None, ALU.logical_shift_right)
                ve.tensor_scalar(dci[1], ci, 4, None, ALU.logical_shift_right)
                ve.tensor_scalar(dci[2], ci, 12, None, ALU.bitwise_and)
                step(ve.tensor_scalar(dci[3], ci, 3, None, ALU.bitwise_and))
                ve.scalar_tensor_tensor(out=ka, in0=dci[0], scalar=-12.0, in1=dci[1], op0=ALU.add, op1=ALU.max)
                step(ve.scalar_tensor_tensor(out=low, in0=ci, scalar=float(CAND_A), in1=dci[2],
                                             op0=ALU.is_lt, op1=ALU.mult))
                step(ve.tensor_tensor(kb, low, dci[3], ALU.add))
                ve.tensor_tensor(eq_b, kb.unsqueeze(2).to_broadcast([P, TB * K, K]), iota16, ALU.is_equal)
                step(ve.tensor_tensor(eq_a, ka.unsqueeze(2).to_broadcast([P, TB * K, K]), iota16, ALU.is_equal))
                ea = eq_a.rearrange("p (t j) a -> p t j a", t=TB)
                eb = eq_b.rearrange("p (t j) a -> p t j a", t=TB)
                ve.tensor_tensor(ea, ea, s_posf[:, 0].unsqueeze(2).to_broadcast([P, TB, K, K]), ALU.mult)
                step(ve.tensor_tensor(eb, eb, s_posf[:, 1].unsqueeze(2).to_broadcast([P, TB, K, K]), ALU.mult))
                ve.tensor_reduce(e1[:, :, bass.ds(h * K, K)], ea, AX.X, ALU.add)
                ve.tensor_reduce(e2[:, :, bass.ds(h * K, K)], eb, AX.X, ALU.add).then_inc(s_e1e2, 1)

            low_input(1, BANKS_H, scale2, bias2)
            add_gate_row(1)
            for j in range(1, 4):
                wait_piece(ve, "wq", j)
                link(head_means(j))
                scaled_means(j)
            with ve.Fori(0, H // 2) as i:
                chain = Chain(ve, s_cl, i, 2 * STEPS_ROUTE)
                route(0, i * 2, chain)
                route(1, i * 2 + 1, chain)
                assert chain.n == 2 * STEPS_ROUTE, chain.n

            link = Chain(ve, s_cs).link
            ve.wait_ge(s_qsd, 1)
            link(ve.reciprocal(pk[:, 1, :], pk[:, 0, :]))
            v4 = vs.rearrange("p t (h k) -> p t h k", h=H)
            w4 = wt.rearrange("p t (h k) -> p t h k", h=H)
            full = [P, TB, H, K]
            link(ve.tensor_tensor(v4, v4, pk[:, 1, :].rearrange("p (h t) -> p t h", h=H).unsqueeze(3).to_broadcast(full),
                                  ALU.mult))
            ve.tensor_tensor(w4, v4, v4[:, :, :, 0:1].to_broadcast(full), ALU.subtract).then_inc(s_shift, 1)
            ve.tensor_copy(key_of, iota.unsqueeze(2).to_broadcast([P, P, TOK]))
            ve.wait_ge(s_exp, 1)
            link(ve.tensor_reduce(pk[:, 2, :].rearrange("p (t h) -> p t h", t=TB), v4, AX.X, ALU.add))
            link(ve.reciprocal(pk[:, 3, :], pk[:, 2, :]))
            ve.tensor_tensor(w4, v4, pk[:, 3, :].rearrange("p (t h) -> p t h", t=TB).unsqueeze(3).to_broadcast(full),
                             ALU.mult).then_inc(s_wt, 1)

            ve.wait_ge(s_scev, 4)
            for b in range(2):
                ve.sem_inc(s_stage[b], 16)
            ve.tensor_copy(wTh, wT).then_inc(s_keyof, 1)
            ve.wait_ge(s_keyof, 1)
            ve.tensor_tensor(wTl, wT, wTh, ALU.subtract).then_inc(s_keyof, 1)
            ve.wait_ge(s_keyof, 2)

            with ve.Fori(0, S // (2 * TOK)) as i:
                a, b = i * (2 * TOK), i * (2 * TOK) + TOK
                ve.wait_ge(s_scmm, i * 4 + 2)
                ve.tensor_tensor(onehot[0], key_of.unsqueeze(1).to_broadcast([P, 2, P, TOK]), both_of(iT, a),
                                 ALU.is_equal).then_inc(s_hot0, 1)
                ve.wait_ge(s_scmm, i * 4 + 4)
                ve.tensor_tensor(onehot[1][:, 0], key_of, of(i1T, b), ALU.is_equal).then_inc(s_hot1, 1)
                ve.wait_ge(s_hot0, i + 1)
                ve.tensor_tensor(gate[0], onehot[0][:, 0:1].to_broadcast([P, 2, P, TOK]), both_of(wThl, a),
                                 ALU.mult).then_inc(s_hot, 1)
                ve.tensor_tensor(onehot[1][:, 1], key_of, of(i2T, b), ALU.is_equal)
                ve.wait_ge(s_hot1, i + 1)
                ve.tensor_tensor(gate[1][:, 0], onehot[1][:, 0], of(wTh, b), ALU.mult).then_inc(s_hot, 1)

            def split_u(i, c):
                ve.wait_ge(s_uhi, i * RT + (c + 1))
                ve.tensor_tensor(u_lo[:, c % GT], u_raw[:, c % RT], u_hi[:, c % GT].bitcast(F32), ALU.subtract
                                 ).then_inc(s_ulo, 1)

            def weigh(i, c, is_early, free):
                s, j, n = c % RT, c % GT, i * RT + c
                if is_early:
                    ve.wait_ge(s_early[s], i * 16 + 16 * (c // RT + 1))
                else:
                    ve.wait_ge(s_act, n + 1)
                g = c // GT
                ve.wait_ge(s_g[g % 2], i * 16 + 16 * (g // 2 + 1))
                made = (early_in[:, s, :] if is_early else gelu_out[:, j, :])
                ve.tensor_tensor(w_full[:, j, :].rearrange("p (b t) -> p b t", b=NST),
                                 made.rearrange("p (b t) -> p b t", b=NST), gate_in[:, g % 2, :, j, :], ALU.mult
                                 ).then_inc(s_w, 1)
                if free is not None:
                    ve.wait_ge(s_vmm, free)
                ve.wait_ge(s_w, n + 1)
                ve.tensor_copy(w_hi[:, s, :], w_full[:, j, :]).then_inc(s_whi, 1)
                ve.wait_ge(s_whi, n + 1)
                ve.tensor_tensor(w_lo[:, s, :], w_full[:, j, :], w_hi[:, s, :].bitcast(F32), ALU.subtract
                                 ).then_inc(s_wlo, 1)

            def add_up(o, n):
                ve.wait_ge(s_vmm, n + 1)
                part = acc[:, o // 2, (o % 2) * 512:(o % 2 + 1) * 512]
                ve.tensor_tensor(part, part, bank[4 + o % 4][:, :], ALU.add).then_inc(s_acc, 1)

            def group(i, g2, first, is_early, ahead, last):
                g = i * 2 + g2
                if not first:
                    ve.wait_ge(s_acc, g * OUTS)
                for j in range(GT):
                    if not last:
                        c = (g2 + 1) * GT + j
                        weigh(i, c, is_early, None if first else g * OUTS)
                        if ahead:
                            split_u(i, c + GT)
                    for o in range(j * OUTS // GT, (j + 1) * OUTS // GT):
                        add_up(o, g * OUTS + o)

            ve.wait_ge(s_scmm, 4 + S // 4)
            for j in range(GT):
                weigh(0, j, True, None)
            ve.wait_ge(s_zacc, 1)
            ve.wait_ge(s_ulo, T_EARLY + GT)
            group(0, 0, True, True, False, False)
            group(0, 1, False, True, False, False)
            with ve.Fori(1, T_EARLY // RT - 1) as i:
                group(i, 0, False, True, False, False)
                group(i, 1, False, True, False, False)
            group(T_EARLY // RT - 1, 0, False, True, False, False)
            group(T_EARLY // RT - 1, 1, False, False, True, False)
            with ve.Fori(T_EARLY // RT, NT // RT - 1) as i:
                group(i, 0, False, False, True, False)
                group(i, 1, False, False, True, False)

            last_sum = (NT // GT - 2) * OUTS
            ve.wait_ge(s_acc, last_sum)
            ve.wait_ge(s_rowg, 4)
            ve.wait_ge(s_x0, 2 * TB)
            ve.wait_ge(s_rows, 96)
            link = Chain(ve, s_cf).link

            for tb in range(TB):
                last = ve.tensor_tensor(acc[:, tb, :], acc[:, tb, :], row_gate[:, :], ALU.mult)
            link(last)
            for tb in range(TB):
                last = ve.scalar_tensor_tensor(out=xt[:, tb, :], in0=xt[:, tb, :], scalar=ALPHA, in1=acc[:, tb, :],
                                               op0=ALU.mult, op1=ALU.add)
            link(last)
            for c in range(GT, RT):
                weigh(NT // RT - 1, c, False, last_sum)
            ve.wait_ge(s_wlo, NT)

            def scale_and_bias(tb):
                ve.wait_ge(s_fsd, tb + 1)
                link(ve.reciprocal(rstd[:, tb:tb + 1], sd[:, tb:tb + 1]))
                ve.scalar_tensor_tensor(out=nmean[:, tb:tb + 1], in0=mv[:, tb, 0:1], scalar=-1.0,
                                        in1=rstd[:, tb:tb + 1], op0=ALU.mult, op1=ALU.mult).then_inc(s_frs, 1)

            for tb in range(TB):
                for half in range(2):
                    o = 2 * tb + half
                    ve.wait_ge(s_vmm, last_sum + o + 1)
                    ve.tensor_tensor(w_full[:, half, :], bank[4 + o % 4][:, :], row_gate[:, half * 512:(half + 1) * 512],
                                     ALU.mult).then_inc(s_acc, 1)
                    piece_x = xt[:, tb, half * 512:(half + 1) * 512]
                    ve.wait_ge(s_acc, last_sum + o + 1)
                    link(ve.tensor_tensor(piece_x, piece_x, w_full[:, half, :], ALU.add))
                    last = ve.bn_stats(st[:, tb, half, :], piece_x)
                link(last)
                ve.bn_aggr(mv[:, tb, :], st[:, tb, :, :]).then_inc(s_ff, 1)
                if tb:
                    scale_and_bias(tb - 1)
            scale_and_bias(TB - 1)
            for tb in range(FIN_POOL, TB):
                ve.wait_ge(s_fnorm, tb + 1)
                link(ve.tensor_tensor(xt[:, tb, :], xt[:, tb, :], row_g[:, :], ALU.mult))
                ve.tensor_tensor(xt[:, tb, :], xt[:, tb, :], row_b[:, :], ALU.add).then_inc(s_fin[tb], 1)


STEPS_ROUTE = 13


def constants():
    import numpy as np

    a = np.zeros((P, NCONST), np.float32)
    a[:, C_ID:C_ID + P] = np.eye(P)
    a[:, C_IOTA:C_IOTA + P] = np.arange(P)
    a[:, C_ONE:C_ONE + P] = 1.0
    a[:, C_MEAN] = 1.0 / DK
    a[:, C_EPS] = LN_EPS
    for g, w in enumerate(WINDOWS):
        for t in range(PAD_P):
            a[:, C_CNT + g * PAD_P + t] = 1.0 / min(t + 1, w)
    return a


def kernel(x, c, ln0_g, ln0_b, ada_w, ada_b, w_in, pool_w, pool_scale, conv_w, conv_b,
           lru_wa, lru_ba, lru_wx, lru_bx, lru_lambda, w_out, ln1_g, ln1_b,
           peer_wq, peer_k1, peer_k2, peer_u, peer_v, ln2_g, ln2_b):
    import numpy as np
    import concourse.bacc as bacc
    from concourse.bass_utils import run_bass_kernel_spmd

    def chunks(a):
        return np.asarray(a).reshape(-1, P).T

    def pieces(w):
        w = np.asarray(w).reshape(KD, P, -1, CHUNK_C)
        return np.ascontiguousarray(w.transpose(2, 1, 0, 3))

    cols = np.concatenate([chunks(a) for a in (
        c, ada_b, ln0_g, ln0_b, ln1_g, ln1_b, pool_scale, conv_b, lru_ba, lru_bx, lru_lambda, conv_w)], axis=1)
    rows = np.stack([np.asarray(a).reshape(D) for a in (
        ln0_g, ln0_b, ln1_g, ln1_b, ln2_g, ln2_b, np.asarray(ada_b)[0, 2 * D:3 * D], np.asarray(ada_b)[0, 5 * D:])])
    arrays = {
        "x": np.asarray(x)[0], "cols": cols, "rows": rows, "consts": constants(),
        "ada_w": pieces(ada_w), "w_in": pieces(w_in), "w_out": pieces(w_out), "wq": pieces(peer_wq),
        "pool_w": np.asarray(pool_w)[0], "wa": np.asarray(lru_wa)[0], "wx": np.asarray(lru_wx)[0],
        "k1t": np.asarray(peer_k1)[0].T, "k2t": np.asarray(peer_k2)[0].T,
        "ut": np.asarray(peer_u)[0].reshape(NT, P, KD, P).transpose(0, 3, 2, 1),
        "v": np.asarray(peer_v)[0].reshape(NT, P, D),
    }
    arrays = {n: np.ascontiguousarray(a) for n, a in arrays.items()}
    nc = bacc.Bacc("TRN2", target_bir_lowering=False, num_devices=1)
    ins = {n: nc.dram_tensor(n + "_dram", a.shape, F32, kind="ExternalInput").ap() for n, a in arrays.items()}
    out = nc.dram_tensor("out_dram", (S, D), F32, kind="ExternalOutput").ap()
    build(nc, *(ins[n] for n in ("x", "cols", "rows", "consts", "ada_w", "w_in", "w_out", "wq", "pool_w",
                                 "wa", "wx", "k1t", "k2t", "ut", "v")), out)
    r = run_bass_kernel_spmd(nc, [{n + "_dram": a for n, a in arrays.items()}], core_ids=[0])
    return r.results[0]["out_dram"].reshape(1, S, D)
```
